# Optimizing a Trainium2 kernel written in Bass

```python
import math
import jax, jax.numpy as jnp
from jax import lax
import numpy as np

D_MODEL = 1024
BATCH = 1
SEQ = 1024
DEPTH = 1

CHUNK = 64
D_MIX = 2 * D_MODEL
SSD_WIDTH = D_MIX // 2
SSD_HEAD_DIM = 64
SSD_HEADS = SSD_WIDTH // SSD_HEAD_DIM
SSD_GROUPS = 2
SSD_STATE = 128
SSD_CONV = 4
SSD_XBC = SSD_WIDTH + 2 * SSD_GROUPS * SSD_STATE
ML_WIDTH = D_MIX - SSD_WIDTH
ML_HEADS = 8
ML_HEAD_DIM = ML_WIDTH // ML_HEADS
ML_CONV = 4
IN_COLS = (SSD_WIDTH + SSD_XBC + SSD_HEADS) + (4 * ML_WIDTH + 2 * ML_HEADS)
MOE_GROUPS = 4
EXPERTS_PER_GROUP = 8
N_EXPERTS = MOE_GROUPS * EXPERTS_PER_GROUP
TOP_K = 2
D_EXPERT = D_MODEL // 2
EPS = 1e-6
STAB_INIT = -1e30


def rmsnorm(x, w):
    xf = x.astype(jnp.float32)
    y = xf * lax.rsqrt(jnp.mean(xf * xf, axis=-1, keepdims=True) + EPS)
    return (y * w.astype(jnp.float32)).astype(x.dtype)

def group_rmsnorm(y, w, groups):
    b, l, c = y.shape
    yg = y.reshape(b, l, groups, c // groups)
    yg = yg * lax.rsqrt(jnp.mean(yg * yg, axis=-1, keepdims=True) + EPS)
    return yg.reshape(b, l, c) * w.astype(jnp.float32)

def causal_dwconv(x, w, b):
    k, c = w.shape
    y = lax.conv_general_dilated(x, w[:, None, :].astype(x.dtype), window_strides=(1,),
                                 padding=[(k - 1, 0)], dimension_numbers=("NWC", "WIO", "NWC"),
                                 feature_group_count=c)
    return y + b.astype(x.dtype)

def ssd_mixer(z, xbc, dt_raw, conv_w, conv_b, dt_bias, a_log, d_skip, norm_w):
    f32 = jnp.float32
    bsz, seq, _ = z.shape
    nc = seq // CHUNK
    r = SSD_HEADS // SSD_GROUPS
    xbc = jax.nn.silu(causal_dwconv(xbc, conv_w, conv_b)).astype(f32)
    xs = xbc[..., :SSD_WIDTH].reshape(bsz, seq, SSD_HEADS, SSD_HEAD_DIM)
    bm = xbc[..., SSD_WIDTH:SSD_WIDTH + SSD_GROUPS * SSD_STATE].reshape(bsz, seq, SSD_GROUPS, SSD_STATE)
    cm = xbc[..., SSD_WIDTH + SSD_GROUPS * SSD_STATE:].reshape(bsz, seq, SSD_GROUPS, SSD_STATE)
    dt = jax.nn.softplus(dt_raw.astype(f32) + dt_bias.astype(f32))
    a = -jnp.exp(a_log.astype(f32))
    xdt = (xs * dt[..., None]).reshape(bsz, nc, CHUNK, SSD_GROUPS, r, SSD_HEAD_DIM)
    xdt = jnp.moveaxis(xdt, 1, 0)
    adt = jnp.transpose((dt * a).reshape(bsz, nc, CHUNK, SSD_GROUPS, r), (1, 0, 3, 4, 2))
    bc = jnp.moveaxis(bm.reshape(bsz, nc, CHUNK, SSD_GROUPS, SSD_STATE), 1, 0)
    cc = jnp.moveaxis(cm.reshape(bsz, nc, CHUNK, SSD_GROUPS, SSD_STATE), 1, 0)
    mask = jnp.tril(jnp.ones((CHUNK, CHUNK), dtype=bool))

    def step(state, inp):
        x_c, a_c, b_c, c_c = inp
        a_cs = jnp.cumsum(a_c, axis=-1)
        seg = jnp.where(mask, a_cs[..., :, None] - a_cs[..., None, :], -jnp.inf)
        lmat = jnp.exp(seg)
        cb = jnp.einsum('blgn,bsgn->bgls', c_c, b_c)
        y = jnp.einsum('bgls,bgrls,bsgrp->blgrp', cb, lmat, x_c)
        y = y + jnp.einsum('blgn,bgrpn,bgrl->blgrp', c_c, state, jnp.exp(a_cs))
        decay = jnp.exp(a_cs[..., -1:] - a_cs)
        state = state * jnp.exp(a_cs[..., -1])[..., None, None] + \
            jnp.einsum('blgn,bgrl,blgrp->bgrpn', b_c, decay, x_c)
        return state, y

    state0 = jnp.zeros((bsz, SSD_GROUPS, r, SSD_HEAD_DIM, SSD_STATE), f32)
    _, y = lax.scan(step, state0, (xdt, adt, bc, cc))
    y = jnp.moveaxis(y, 0, 1).reshape(bsz, seq, SSD_HEADS, SSD_HEAD_DIM)
    y = y + d_skip.astype(f32)[:, None] * xs
    y = y.reshape(bsz, seq, SSD_WIDTH) * jax.nn.silu(z.astype(f32))
    return group_rmsnorm(y, norm_w, SSD_GROUPS).astype(z.dtype)

def mlstm_mixer(qk, v, o_pre, i_pre, f_pre, conv_w, conv_b, i_bias, f_bias, norm_w):
    f32 = jnp.float32
    bsz, seq, _ = v.shape
    nc = seq // CHUNK
    qk = jax.nn.silu(causal_dwconv(qk, conv_w, conv_b)).astype(f32)
    shp = (bsz, nc, CHUNK, ML_HEADS, ML_HEAD_DIM)
    q = jnp.moveaxis(qk[..., :ML_WIDTH].reshape(shp), 1, 0)
    k = jnp.moveaxis(qk[..., ML_WIDTH:].reshape(shp), 1, 0) * (ML_HEAD_DIM ** -0.5)
    vv = jnp.moveaxis(v.astype(f32).reshape(shp), 1, 0)
    ig = i_pre.astype(f32) + i_bias.astype(f32)
    lf = jax.nn.log_sigmoid(f_pre.astype(f32) + f_bias.astype(f32))
    ig = jnp.transpose(ig.reshape(bsz, nc, CHUNK, ML_HEADS), (1, 0, 3, 2))
    lf = jnp.transpose(lf.reshape(bsz, nc, CHUNK, ML_HEADS), (1, 0, 3, 2))
    mask = jnp.tril(jnp.ones((CHUNK, CHUNK), dtype=bool))

    def step(carry, inp):
        cmem, nmem, m = carry
        q_c, k_c, v_c, i_c, f_c = inp
        bcum = jnp.cumsum(f_c, axis=-1)
        dmat = jnp.where(mask, bcum[..., :, None] - bcum[..., None, :] + i_c[..., None, :], -jnp.inf)
        m_inter = bcum + m[..., None]
        m_t = jnp.maximum(m_inter, jnp.max(dmat, axis=-1))
        w = jnp.exp(dmat - m_t[..., None])
        s = jnp.einsum('blhd,bshd->bhls', q_c, k_c) * w
        inter = jnp.exp(m_inter - m_t)
        num = jnp.einsum('bhls,bshv->blhv', s, v_c) + \
            jnp.einsum('blhk,bhkv->blhv', q_c, cmem) * jnp.swapaxes(inter, 1, 2)[..., None]
        den = jnp.sum(s, axis=-1) + inter * jnp.einsum('blhk,bhk->bhl', q_c, nmem)
        den = jnp.maximum(jnp.abs(den), jnp.exp(-m_t))
        h = num / jnp.swapaxes(den, 1, 2)[..., None]
        g = bcum[..., -1]
        a = g[..., None] - bcum + i_c
        m_new = jnp.maximum(g + m, jnp.max(a, axis=-1))
        wc = jnp.exp(a - m_new[..., None])
        carry_scale = jnp.exp(g + m - m_new)
        cmem = cmem * carry_scale[..., None, None] + jnp.einsum('bhs,bshk,bshv->bhkv', wc, k_c, v_c)
        nmem = nmem * carry_scale[..., None] + jnp.einsum('bhs,bshk->bhk', wc, k_c)
        return (cmem, nmem, m_new), h

    carry0 = (jnp.zeros((bsz, ML_HEADS, ML_HEAD_DIM, ML_HEAD_DIM), f32),
              jnp.zeros((bsz, ML_HEADS, ML_HEAD_DIM), f32),
              jnp.full((bsz, ML_HEADS), STAB_INIT, f32))
    _, h = lax.scan(step, carry0, (q, k, vv, ig, lf))
    h = jnp.moveaxis(h, 0, 1).reshape(bsz, seq, ML_HEADS, ML_HEAD_DIM)
    mu = jnp.mean(h, axis=-1, keepdims=True)
    var = jnp.mean((h - mu) ** 2, axis=-1, keepdims=True)
    h = ((h - mu) * lax.rsqrt(var + EPS)).reshape(bsz, seq, ML_WIDTH) * norm_w.astype(f32)
    h = jax.nn.sigmoid(o_pre.astype(f32)) * h
    return h.astype(v.dtype)

def hier_moe(h, wg, bg, we, be, w_gate, w_up, w_down):
    bsz, seq, d = h.shape
    t = bsz * seq
    xf = h.reshape(t, d)
    x32 = xf.astype(jnp.float32)
    p_group = jax.nn.softmax(x32 @ wg.astype(jnp.float32) + bg.astype(jnp.float32), axis=-1)
    pg, g_sel = lax.top_k(p_group, 1)
    e_logits = (x32 @ we.astype(jnp.float32) + be.astype(jnp.float32)).reshape(t, MOE_GROUPS, EXPERTS_PER_GROUP)
    e_in = jnp.take_along_axis(e_logits, g_sel[:, :, None], axis=1)[:, 0]
    top_v, top_i = lax.top_k(e_in, TOP_K)
    gates = jax.nn.softmax(top_v, axis=-1) * pg
    ids = (g_sel * EXPERTS_PER_GROUP + top_i).reshape(-1).astype(jnp.int32)
    order = jnp.argsort(ids)
    tok = order // TOP_K
    xs = xf[tok]
    sizes = jnp.bincount(ids, length=N_EXPERTS).astype(jnp.int32)
    hg = lax.ragged_dot(xs, w_gate.astype(xs.dtype), sizes)
    hu = lax.ragged_dot(xs, w_up.astype(xs.dtype), sizes)
    ys = lax.ragged_dot(jax.nn.silu(hg) * hu, w_down.astype(xs.dtype), sizes)
    ys = ys * gates.reshape(-1)[order][:, None].astype(ys.dtype)
    y = jax.ops.segment_sum(ys, tok, num_segments=t)
    return y.reshape(bsz, seq, d).astype(h.dtype)

def first_inputs(seed: int = 0) -> dict:
    key = jax.random.key(seed)
    ks = jax.random.split(key, 26)
    nrm = lambda k, s, sc: jax.random.normal(k, s, jnp.float32) * sc
    dt0 = jnp.exp(jax.random.uniform(ks[6], (DEPTH, SSD_HEADS), jnp.float32, math.log(1e-3), math.log(1e-1)))
    return {
        "x": jax.random.normal(ks[0], (BATCH, SEQ, D_MODEL), jnp.float32),
        "norm1_w": 1.0 + nrm(ks[1], (DEPTH, D_MODEL), 0.02),
        "w_in": nrm(ks[2], (DEPTH, D_MODEL, IN_COLS), D_MODEL ** -0.5),
        "ssd_conv_w": nrm(ks[3], (DEPTH, SSD_CONV, SSD_XBC), SSD_CONV ** -0.5),
        "ssd_conv_b": nrm(ks[4], (DEPTH, SSD_XBC), 0.02),
        "ssd_dt_bias": dt0 + jnp.log(-jnp.expm1(-dt0)),
        "ssd_a_log": jnp.log(jax.random.uniform(ks[5], (DEPTH, SSD_HEADS), jnp.float32, 1.0, 16.0)),
        "ssd_d": 1.0 + nrm(ks[7], (DEPTH, SSD_HEADS), 0.1),
        "ssd_norm_w": 1.0 + nrm(ks[8], (DEPTH, SSD_WIDTH), 0.02),
        "ml_conv_w": nrm(ks[9], (DEPTH, ML_CONV, 2 * ML_WIDTH), ML_CONV ** -0.5),
        "ml_conv_b": nrm(ks[10], (DEPTH, 2 * ML_WIDTH), 0.02),
        "ml_i_bias": nrm(ks[11], (DEPTH, ML_HEADS), 0.1),
        "ml_f_bias": 3.0 + 3.0 * jax.random.uniform(ks[12], (DEPTH, ML_HEADS), jnp.float32),
        "ml_norm_w": 1.0 + nrm(ks[13], (DEPTH, ML_WIDTH), 0.02),
        "w_out": nrm(ks[14], (DEPTH, D_MIX, D_MODEL), D_MIX ** -0.5),
        "norm2_w": 1.0 + nrm(ks[15], (DEPTH, D_MODEL), 0.02),
        "router_g_w": nrm(ks[16], (DEPTH, D_MODEL, MOE_GROUPS), D_MODEL ** -0.5),
        "router_g_b": nrm(ks[17], (DEPTH, MOE_GROUPS), 0.01),
        "router_e_w": nrm(ks[18], (DEPTH, D_MODEL, N_EXPERTS), D_MODEL ** -0.5),
        "router_e_b": nrm(ks[19], (DEPTH, N_EXPERTS), 0.01),
        "exp_w_gate": nrm(ks[20], (DEPTH, N_EXPERTS, D_MODEL, D_EXPERT), D_MODEL ** -0.5),
        "exp_w_up": nrm(ks[21], (DEPTH, N_EXPERTS, D_MODEL, D_EXPERT), D_MODEL ** -0.5),
        "exp_w_down": nrm(ks[22], (DEPTH, N_EXPERTS, D_EXPERT, D_MODEL), D_EXPERT ** -0.5),
        "norm_f_w": 1.0 + nrm(ks[23], (D_MODEL,), 0.02),
    }

def first_block(x, norm1_w, w_in, ssd_conv_w, ssd_conv_b, ssd_dt_bias, ssd_a_log, ssd_d, ssd_norm_w,
              ml_conv_w, ml_conv_b, ml_i_bias, ml_f_bias, ml_norm_w, w_out, norm2_w,
              router_g_w, router_g_b, router_e_w, router_e_b, exp_w_gate, exp_w_up, exp_w_down, norm_f_w):
    o1 = SSD_WIDTH
    o2 = o1 + SSD_XBC
    o3 = o2 + SSD_HEADS
    o4 = o3 + 2 * ML_WIDTH
    o5 = o4 + ML_WIDTH
    o6 = o5 + ML_WIDTH
    o7 = o6 + ML_HEADS
    for layer in range(DEPTH):
        h = rmsnorm(x, norm1_w[layer])
        p = jnp.einsum('bsd,de->bse', h, w_in[layer])
        y_ssd = ssd_mixer(p[..., :o1], p[..., o1:o2], p[..., o2:o3],
                          ssd_conv_w[layer], ssd_conv_b[layer], ssd_dt_bias[layer],
                          ssd_a_log[layer], ssd_d[layer], ssd_norm_w[layer])
        y_ml = mlstm_mixer(p[..., o3:o4], p[..., o4:o5], p[..., o5:o6], p[..., o6:o7], p[..., o7:],
                           ml_conv_w[layer], ml_conv_b[layer], ml_i_bias[layer], ml_f_bias[layer],
                           ml_norm_w[layer])
        mix = jnp.concatenate([y_ssd, y_ml], axis=-1)
        x = x + jnp.einsum('bse,ed->bsd', mix, w_out[layer])
        h2 = rmsnorm(x, norm2_w[layer])
        x = x + hier_moe(h2, router_g_w[layer], router_g_b[layer], router_e_w[layer], router_e_b[layer],
                         exp_w_gate[layer], exp_w_up[layer], exp_w_down[layer])
    return rmsnorm(x, norm_f_w)


HY_WIDTH = 512
HY_GROUPS = 8
HY_ORDER = 2
HY_EMB = 33
HY_BANDS = (HY_EMB - 1) // 2
HY_FILT_HIDDEN = 64
HY_FAST_DECAY = 0.3
HY_SLOW_DECAY = 1.5
HY_DECAY_TARGET = 1e-2
HY_MAX_DECAY = math.log(HY_DECAY_TARGET) / HY_FAST_DECAY
HY_MIN_DECAY = math.log(HY_DECAY_TARGET) / HY_SLOW_DECAY
HY_COLS = 3 * HY_WIDTH

RW_WIDTH = 512
RW_HEAD = 64
RW_HEADS = RW_WIDTH // RW_HEAD
RW_LORA_W = 64
RW_LORA_A = 64
RW_LORA_G = 128
RW_GN_EPS = 64e-5
RW_SIZES = [RW_WIDTH, RW_WIDTH, RW_WIDTH, RW_LORA_W, RW_LORA_W, RW_LORA_A, RW_LORA_A, RW_LORA_G]
RW_OFFSETS = [sum(RW_SIZES[:i + 1]) for i in range(len(RW_SIZES) - 1)]
RW_COLS = sum(RW_SIZES)

GATE_COLS = 2 * D_MODEL
IN_COLS_2 = HY_COLS + RW_COLS + GATE_COLS

FFN_HIDDEN = ((8 * D_MODEL + 3 * 256 - 1) // (3 * 256)) * 256

DN_ALPHA = (2.0 * DEPTH) ** 0.25
DN_BETA = (8.0 * DEPTH) ** -0.25
LN_EPS = 1e-5


def layer_norm(x, w, b):
    xf = x.astype(jnp.float32)
    mu = jnp.mean(xf, axis=-1, keepdims=True)
    var = jnp.mean(jnp.square(xf - mu), axis=-1, keepdims=True)
    return ((xf - mu) * lax.rsqrt(var + LN_EPS) * w + b).astype(x.dtype)

def shift_prev(z):
    return jnp.pad(z[:, :-1], ((0, 0), (1, 0), (0, 0)))

def shift_next(z):
    return jnp.pad(z[:, 1:], ((0, 0), (0, 1), (0, 0)))

def short_conv3(z, w, b):
    return w[0] * shift_prev(z) + w[1] * z + w[2] * shift_next(z) + b

def hyena_filters(L, fw1, fb1, fw2, fb2, fw3, fb3, fw4, sin_freq):
    f32 = jnp.float32
    t = jnp.linspace(0.0, 1.0, L, dtype=f32)[:, None]
    w = 2.0 * math.pi * jnp.arange(L, dtype=f32) / L
    f = jnp.linspace(1e-4, HY_BANDS - 1, HY_BANDS, dtype=f32)
    ang = w[:, None] * f[None, :]
    feats = jnp.concatenate([t, jnp.cos(ang), -jnp.sin(ang)], axis=-1)
    sf = sin_freq.astype(f32)
    h = jnp.sin(sf[0] * (feats @ fw1.astype(f32) + fb1.astype(f32)))
    h = jnp.sin(sf[1] * (h @ fw2.astype(f32) + fb2.astype(f32)))
    h = jnp.sin(sf[2] * (h @ fw3.astype(f32) + fb3.astype(f32)))
    h = (h @ fw4.astype(f32)).reshape(L, HY_ORDER, 2, HY_WIDTH)
    deltas = jnp.abs(jnp.linspace(HY_MIN_DECAY, HY_MAX_DECAY, HY_WIDTH, dtype=f32))
    window = jnp.exp(-t * deltas[None, :])
    return h * window[:, None, None, :]

def long_conv(z, h_fwd, h_bwd, d_skip):
    L = z.shape[1]
    n = 2 * L
    zf = jnp.fft.rfft(z, n=n, axis=1)
    hf = jnp.fft.rfft(h_fwd, n=n, axis=0) + jnp.conj(jnp.fft.rfft(h_bwd, n=n, axis=0))
    y = jnp.fft.irfft(zf * hf[None], n=n, axis=1)[:, :L]
    return y + z * d_skip

def hyena_mixer(u, conv_w, conv_b, fw1, fb1, fw2, fb2, fw3, fb3, fw4, sin_freq, skip):
    L = u.shape[1]
    u = short_conv3(u, conv_w, conv_b).astype(jnp.float32)
    v, x1, x2 = jnp.split(u, 3, axis=-1)
    h = hyena_filters(L, fw1, fb1, fw2, fb2, fw3, fb3, fw4, sin_freq)
    sk = skip.astype(jnp.float32)
    z = x1 * long_conv(v, h[:, 0, 0], h[:, 0, 1], sk[0])
    z = x2 * long_conv(z, h[:, 1, 0], h[:, 1, 1], sk[1])
    return z

def rwkv_step(S, inp):
    r, w, k, v, kk, a = inp
    sa = jnp.einsum('dbhvk,dbhk->dbhv', S, -kk)
    S = S * w[..., None, :] + sa[..., :, None] * (kk * a)[..., None, :] + v[..., :, None] * k[..., None, :]
    y = jnp.einsum('dbhvk,dbhk->dbhv', S, r)
    return S, y

def rwkv_mixer(u, mu, w0, w2, a0, a2, g2, k_k, k_a, r_k, gn_w, gn_b):
    f32 = jnp.float32
    B, L, _ = u.shape
    u = u + mu * (0.5 * (shift_prev(u) + shift_next(u)) - u)
    r, k, v, wd_f, wd_b, ad_f, ad_b, gd = jnp.split(u.astype(f32), RW_OFFSETS, axis=-1)
    d = w0.astype(f32)[:, None, None, :] + jnp.einsum('dblr,drc->dblc', jnp.tanh(jnp.stack([wd_f, wd_b])), w2.astype(f32))
    decay = jnp.exp(-math.exp(-0.5) * jax.nn.sigmoid(d))
    a = jax.nn.sigmoid(a0.astype(f32)[:, None, None, :] + jnp.einsum('dblr,drc->dblc', jnp.stack([ad_f, ad_b]), a2.astype(f32)))
    g = jax.nn.sigmoid(gd) @ g2.astype(f32)

    def heads(z):
        return z.reshape(z.shape[:-1] + (RW_HEADS, RW_HEAD))

    kk = heads(k * k_k.astype(f32))
    kk = kk / jnp.maximum(jnp.sqrt(jnp.sum(kk * kk, axis=-1, keepdims=True)), 1e-12)
    kd = heads(k[None] * (1.0 + (a - 1.0) * k_a.astype(f32)))
    r_h, v_h, w_h, a_h = heads(r), heads(v), heads(decay), heads(a)

    def dirs(z_f, z_b):
        return jnp.moveaxis(jnp.stack([z_f, z_b[:, ::-1]]), 2, 0)

    xs = (dirs(r_h, r_h), dirs(w_h[0], w_h[1]), dirs(kd[0], kd[1]),
          dirs(v_h, v_h), dirs(kk, kk), dirs(a_h[0], a_h[1]))
    S0 = jnp.zeros((2, B, RW_HEADS, RW_HEAD, RW_HEAD), f32)
    _, ys = lax.scan(rwkv_step, S0, xs)
    ys = jnp.moveaxis(ys, 0, 2)
    y = ys[0] + ys[1][:, ::-1]
    mu_y = jnp.mean(y, axis=-1, keepdims=True)
    var_y = jnp.mean(jnp.square(y - mu_y), axis=-1, keepdims=True)
    y = (y - mu_y) * lax.rsqrt(var_y + RW_GN_EPS) * heads(gn_w.astype(f32)) + heads(gn_b.astype(f32))
    bonus = jnp.sum(r_h[None] * kd * r_k.astype(f32), axis=-1, keepdims=True) * v_h[None]
    y = y + jnp.sum(bonus, axis=0)
    return y.reshape(B, L, RW_WIDTH) * g

def hybrid_layer(x, w_in, hy_conv_w, hy_conv_b, hy_filt_w1, hy_filt_b1, hy_filt_w2, hy_filt_b2,
                 hy_filt_w3, hy_filt_b3, hy_filt_w4, hy_sin_freq, hy_skip, rw_mu, rw_w0, rw_w2,
                 rw_a0, rw_a2, rw_g2, rw_k_k, rw_k_a, rw_r_k, rw_gn_w, rw_gn_b, w_hy_out, w_rw_out,
                 w_o, ln1_w, ln1_b, ffn_w_gate, ffn_w_up, ffn_w_down, ln2_w, ln2_b):
    dt = x.dtype
    proj = x @ w_in
    u_h, u_r, gates = jnp.split(proj, [HY_COLS, HY_COLS + RW_COLS], axis=-1)
    y_h = hyena_mixer(u_h, hy_conv_w, hy_conv_b, hy_filt_w1, hy_filt_b1, hy_filt_w2, hy_filt_b2,
                      hy_filt_w3, hy_filt_b3, hy_filt_w4, hy_sin_freq, hy_skip).astype(dt) @ w_hy_out
    y_r = rwkv_mixer(u_r, rw_mu, rw_w0, rw_w2, rw_a0, rw_a2, rw_g2, rw_k_k, rw_k_a, rw_r_k,
                     rw_gn_w, rw_gn_b).astype(dt) @ w_rw_out
    g_h, g_r = jnp.split(jax.nn.sigmoid(gates), 2, axis=-1)
    mix = (g_h * y_h + g_r * y_r) @ w_o
    x = layer_norm(DN_ALPHA * x + mix, ln1_w, ln1_b)
    ffn = (jax.nn.silu(x @ ffn_w_gate) * (x @ ffn_w_up)) @ ffn_w_down
    return layer_norm(DN_ALPHA * x + ffn, ln2_w, ln2_b)

def second_inputs(seed: int = 0) -> dict:
    key = jax.random.key(seed)
    keys = iter(jax.random.split(key, 48))

    def nrm(shape, scale):
        return jax.random.normal(next(keys), shape, jnp.float32) * scale

    Ld = DEPTH
    return {
        "x": nrm((BATCH, SEQ, D_MODEL), 1.0),
        "w_in": nrm((Ld, D_MODEL, IN_COLS_2), D_MODEL ** -0.5),
        "hy_conv_w": nrm((Ld, 3, HY_COLS), 3 ** -0.5),
        "hy_conv_b": nrm((Ld, HY_COLS), 0.02),
        "hy_filt_w1": nrm((Ld, HY_EMB, HY_FILT_HIDDEN), HY_EMB ** -0.5),
        "hy_filt_b1": nrm((Ld, HY_FILT_HIDDEN), 0.1),
        "hy_filt_w2": nrm((Ld, HY_FILT_HIDDEN, HY_FILT_HIDDEN), HY_FILT_HIDDEN ** -0.5),
        "hy_filt_b2": nrm((Ld, HY_FILT_HIDDEN), 0.1),
        "hy_filt_w3": nrm((Ld, HY_FILT_HIDDEN, HY_FILT_HIDDEN), HY_FILT_HIDDEN ** -0.5),
        "hy_filt_b3": nrm((Ld, HY_FILT_HIDDEN), 0.1),
        "hy_filt_w4": nrm((Ld, HY_FILT_HIDDEN, HY_ORDER * 2 * HY_WIDTH), 0.1 * HY_FILT_HIDDEN ** -0.5),
        "hy_sin_freq": 1.0 + nrm((Ld, 3, HY_FILT_HIDDEN), 0.05),
        "hy_skip": nrm((Ld, HY_ORDER, HY_WIDTH), 0.5),
        "rw_mu": 0.5 + nrm((Ld, RW_COLS), 0.1),
        "rw_w0": -0.5 + nrm((Ld, 2, RW_WIDTH), 0.5),
        "rw_w2": nrm((Ld, 2, RW_LORA_W, RW_WIDTH), 0.5 * RW_LORA_W ** -0.5),
        "rw_a0": nrm((Ld, 2, RW_WIDTH), 0.1),
        "rw_a2": nrm((Ld, 2, RW_LORA_A, RW_WIDTH), 0.5 * RW_LORA_A ** -0.5),
        "rw_g2": nrm((Ld, RW_LORA_G, RW_WIDTH), RW_LORA_G ** -0.5),
        "rw_k_k": 0.85 + nrm((Ld, RW_WIDTH), 0.05),
        "rw_k_a": 1.0 + nrm((Ld, RW_WIDTH), 0.05),
        "rw_r_k": nrm((Ld, RW_HEADS, RW_HEAD), 0.1),
        "rw_gn_w": 1.0 + nrm((Ld, RW_WIDTH), 0.05),
        "rw_gn_b": nrm((Ld, RW_WIDTH), 0.02),
        "w_hy_out": nrm((Ld, HY_WIDTH, D_MODEL), HY_WIDTH ** -0.5),
        "w_rw_out": nrm((Ld, RW_WIDTH, D_MODEL), RW_WIDTH ** -0.5),
        "w_o": nrm((Ld, D_MODEL, D_MODEL), DN_BETA * D_MODEL ** -0.5),
        "ln1_w": 1.0 + nrm((Ld, D_MODEL), 0.05),
        "ln1_b": nrm((Ld, D_MODEL), 0.02),
        "ffn_w_gate": nrm((Ld, D_MODEL, FFN_HIDDEN), D_MODEL ** -0.5),
        "ffn_w_up": nrm((Ld, D_MODEL, FFN_HIDDEN), D_MODEL ** -0.5),
        "ffn_w_down": nrm((Ld, FFN_HIDDEN, D_MODEL), DN_BETA * FFN_HIDDEN ** -0.5),
        "ln2_w": 1.0 + nrm((Ld, D_MODEL), 0.05),
        "ln2_b": nrm((Ld, D_MODEL), 0.02),
    }

def second_block(x, w_in, hy_conv_w, hy_conv_b, hy_filt_w1, hy_filt_b1, hy_filt_w2, hy_filt_b2,
              hy_filt_w3, hy_filt_b3, hy_filt_w4, hy_sin_freq, hy_skip, rw_mu, rw_w0, rw_w2,
              rw_a0, rw_a2, rw_g2, rw_k_k, rw_k_a, rw_r_k, rw_gn_w, rw_gn_b, w_hy_out, w_rw_out,
              w_o, ln1_w, ln1_b, ffn_w_gate, ffn_w_up, ffn_w_down, ln2_w, ln2_b):
    for l in range(DEPTH):
        x = hybrid_layer(x, w_in[l], hy_conv_w[l], hy_conv_b[l], hy_filt_w1[l], hy_filt_b1[l],
                         hy_filt_w2[l], hy_filt_b2[l], hy_filt_w3[l], hy_filt_b3[l], hy_filt_w4[l],
                         hy_sin_freq[l], hy_skip[l], rw_mu[l], rw_w0[l], rw_w2[l], rw_a0[l],
                         rw_a2[l], rw_g2[l], rw_k_k[l], rw_k_a[l], rw_r_k[l], rw_gn_w[l], rw_gn_b[l],
                         w_hy_out[l], w_rw_out[l], w_o[l], ln1_w[l], ln1_b[l], ffn_w_gate[l],
                         ffn_w_up[l], ffn_w_down[l], ln2_w[l], ln2_b[l])
    return x


def setup_inputs(seed=0):
    out = dict(first_inputs(seed))
    for name, value in second_inputs(seed + 1).items():
        if name != "x":
            out[name + "_2"] = value
    return out


def reference(
    x, norm1_w, w_in, ssd_conv_w, ssd_conv_b, ssd_dt_bias, ssd_a_log, ssd_d, ssd_norm_w,
    ml_conv_w, ml_conv_b, ml_i_bias, ml_f_bias, ml_norm_w, w_out, norm2_w, router_g_w,
    router_g_b, router_e_w, router_e_b, exp_w_gate, exp_w_up, exp_w_down, norm_f_w, w_in_2,
    hy_conv_w_2, hy_conv_b_2, hy_filt_w1_2, hy_filt_b1_2, hy_filt_w2_2, hy_filt_b2_2,
    hy_filt_w3_2, hy_filt_b3_2, hy_filt_w4_2, hy_sin_freq_2, hy_skip_2, rw_mu_2, rw_w0_2,
    rw_w2_2, rw_a0_2, rw_a2_2, rw_g2_2, rw_k_k_2, rw_k_a_2, rw_r_k_2, rw_gn_w_2, rw_gn_b_2,
    w_hy_out_2, w_rw_out_2, w_o_2, ln1_w_2, ln1_b_2, ffn_w_gate_2, ffn_w_up_2, ffn_w_down_2,
    ln2_w_2, ln2_b_2,
):
    x = first_block(
        x, norm1_w, w_in, ssd_conv_w, ssd_conv_b, ssd_dt_bias, ssd_a_log, ssd_d, ssd_norm_w,
        ml_conv_w, ml_conv_b, ml_i_bias, ml_f_bias, ml_norm_w, w_out, norm2_w, router_g_w,
        router_g_b, router_e_w, router_e_b, exp_w_gate, exp_w_up, exp_w_down, norm_f_w,
    )
    return second_block(
        x, w_in_2, hy_conv_w_2, hy_conv_b_2, hy_filt_w1_2, hy_filt_b1_2, hy_filt_w2_2,
        hy_filt_b2_2, hy_filt_w3_2, hy_filt_b3_2, hy_filt_w4_2, hy_sin_freq_2, hy_skip_2,
        rw_mu_2, rw_w0_2, rw_w2_2, rw_a0_2, rw_a2_2, rw_g2_2, rw_k_k_2, rw_k_a_2, rw_r_k_2,
        rw_gn_w_2, rw_gn_b_2, w_hy_out_2, w_rw_out_2, w_o_2, ln1_w_2, ln1_b_2, ffn_w_gate_2,
        ffn_w_up_2, ffn_w_down_2, ln2_w_2, ln2_b_2,
    )


_drawn_inputs = setup_inputs


def setup_inputs(seed=0):
    import zlib

    import numpy as np

    out = dict(_drawn_inputs(seed))
    spreads = {}
    factors = {'ssd_norm_w': 2.738,
     'ml_conv_b': 3.201,
     'ml_i_bias': 64.0,
     'ml_norm_w': 3.235,
     'router_g_b': 13.501,
     'router_e_b': 4.642,
     'rw_w2_2': 5.351,
     'rw_a0_2': 8.0,
     'rw_k_k_2': 25.177,
     'rw_k_a_2': 4.755,
     'rw_gn_w_2': 8.0,
     'rw_gn_b_2': 30.002,
     'ln1_b_2': 2.794,
     'ln2_b_2': 2.881,
     'norm2_w': 2.953,
     'hy_conv_b_2': 3.834,
     'hy_sin_freq_2': 3.174}
    for name, (base, spread) in spreads.items():
        noise = np.random.default_rng([zlib.crc32(name.encode()), seed]).standard_normal(out[name].shape)
        drawn = base * np.exp(spread * noise) if base else spread * noise
        out[name] = __import__('jax').numpy.asarray(drawn.astype(out[name].dtype))
    for name, factor in factors.items():
        out[name] = (out[name] * factor).astype(out[name].dtype)
    return out
```

```python
from contextlib import ExitStack

import numpy as np

import concourse.bass as bass
from concourse import mybir

F32 = mybir.dt.float32
U32 = mybir.dt.uint32
I32 = mybir.dt.int32
HALF = mybir.dt.float32r
ACT = mybir.ActivationFunctionType
ALU = mybir.AluOpType
AXX = mybir.AxisListType.X

P = 128
SEQ = 1024
D = 1024
NT = SEQ // P
BIG = 1e30
EPS = 1e-6

CHUNK = 128
NCH = SEQ // CHUNK
SSD_H, SSD_P, SSD_G, SSD_N = 16, 64, 2, 128
SSD_W = SSD_H * SSD_P
XBC = SSD_W + 2 * SSD_G * SSD_N
ML_H, ML_D = 8, 128
ML_W = ML_H * ML_D
CONV1 = XBC + 2 * ML_W
O_XBC = SSD_W
O_DT = O_XBC + XBC
O_QK = O_DT + SSD_H
O_V = O_QK + 2 * ML_W
O_O = O_V + ML_W
O_IF = O_O + ML_W
MIX_W = SSD_W + ML_W
N_GROUP, PER_GROUP = 4, 8
N_EXP = N_GROUP * PER_GROUP
D_EXP = 512
N_TILE = N_EXP + (2 * SEQ - N_EXP) // P
N_LIST = N_TILE + 2
N_SLOT = N_LIST * P
HY_W = 512
RW_W, RW_H, RW_D = 512, 8, 64
RW_COLS = 3 * RW_W + 4 * 64 + 128
HY_COLS = 3 * HY_W
CONV2 = HY_COLS + RW_COLS
FFN_H = 2816
DN_ALPHA = 2.0 ** 0.25
LN_EPS = 1e-5
RW_GN_EPS = 64e-5
NF = 2 * SEQ


class Stage:

    def __init__(self, nc, name):
        self.nc, self.name, self.stack, self.sems = nc, name, ExitStack(), []

    def __enter__(self):
        return self

    def __exit__(self, kind, *rest):
        self.stack.__exit__(kind, *rest)
        if kind is None:
            self.nc.clear_and_free_semaphores(self.sems)
            self.nc.all_engine_barrier()

    def sb(self, name, shape, dt=F32):
        return self.stack.enter_context(self.nc.sbuf_tensor(f"{self.name}_{name}", shape, dt))

    def ps(self, name, shape, dt=F32):
        return self.stack.enter_context(self.nc.psum_tensor(f"{self.name}_{name}", shape, dt))

    def sem(self, name):
        self.sems.append(self.nc.alloc_semaphore(f"{self.name}_{name}"))
        return self.sems[-1]

    def block(self):
        return self.stack.enter_context(self.nc.Block())


def rows(ap):
    return ap.rearrange("(t p) n -> p t n", p=P)


def bc(ap, shape):
    return ap.to_broadcast(shape)


def products3(pe, out, l, r, k, kt):
    pe.matmul(out, l[1], r[0], start=(k == 0), stop=False)
    pe.matmul(out, l[0], r[1], start=False, stop=False)
    return pe.matmul(out, l[0], r[0], start=False, stop=(k == kt - 1))


def halves_on_pool(pool, x, hi, lo, one, shape):
    ones = one[:, :]
    while len(ones.shape) < len(shape):
        ones = ones.unsqueeze(2)
    pool.tensor_tensor(hi, x, bc(ones, shape), ALU.mult)
    pool.drain()
    return pool.tensor_tensor(lo, x, hi, ALU.subtract)


def small_gemm(nc, name, a_half, kt, w_sb, ident, out):
    n = w_sb.shape[2]
    with Stage(nc, name) as s:
        p_t, ps, oT = s.ps("p_t", [n, 2, 512]), s.ps("ps", [P, NT, 64]), s.sb("oT", [n, SEQ])
        w_hi, w_lo = (s.sb(q, [P, kt, n], HALF) for q in ("w_hi", "w_lo"))
        split, multiplied, copied, done = (s.sem(q) for q in ("split", "multiplied", "copied", "done"))
        block = s.block()

        @block.tensor
        def _(pe):
            pe.wait_ge(split, 1)
            for h in range(2):
                for k in range(kt):
                    mm = products3(pe, p_t[:, h], (w_hi[:, k], w_lo[:, k]),
                                   [a[:, k, h * 512:h * 512 + 512] for a in a_half], k, kt)
                mm.then_inc(multiplied, 1)
            for t in range(NT):
                pe.wait_ge(copied, t // 4 + 1)
                mm = pe.transpose(ps[:, t, 0:n], oT[:, t * P:t * P + P], ident[0:n, 0:n])
            mm.then_inc(done, 1)

        @block.vector
        def _(v):
            v.tensor_copy(w_hi[:, :, :], w_sb[:, :, :])
            v.drain()
            v.tensor_tensor(w_lo[:, :, :], w_sb[:, :, :], w_hi[:, :, :], ALU.subtract).then_inc(split, 1)
            for h in range(2):
                v.wait_ge(multiplied, h + 1)
                v.tensor_copy(oT[:, h * 512:h * 512 + 512], p_t[:, h]).then_inc(copied, 1)
            v.wait_ge(done, 1)
            v.tensor_copy(out[:, :, :], ps[:, :, 0:n])


def gemm(nc, name, a_half, kt, segs, clear=None):
    NB = 512
    has_conv = segs[0]["kind"] == "conv"
    taps = segs[0]["taps"] if has_conv else 0
    with Stage(nc, name) as s:
        w_sb, one = s.sb("w", [P, kt, NB]), s.sb("one", [P, 1])
        w_hi, w_lo = (s.sb(n, [P, 2, kt, NB], HALF) for n in ("w_hi", "w_lo"))
        a_hi, a_lo = a_half
        st = s.sb("st", [P, 2, 8, NB])
        ps = s.ps("ps", [P, 8, NB])
        if has_conv:
            pad, par, sig = s.sb("pad", [P, 2, SEQ + 4]), s.sb("par", [P, 2, 4, taps + 2]), s.sb("sig", [P, 2, SEQ])
        if clear is not None:
            zero, zeroed = s.sb("zero", [P, D]), s.sem("zeroed")
        w_in = s.sem("w_in")
        par_in = [s.sem(f"par_in{b}") for b in range(2)]
        stored = [s.sem(f"stored{b}") for b in range(2)]
        products, by_act, by_dve, cleared, summed, sigmoid, gated, split = (
            s.sem(n) for n in ("products", "by_act", "by_dve", "cleared", "summed", "sigmoid", "gated", "split"))
        block = s.block()
        n_all = sum(g["w"].shape[1] // NB for g in segs)

        def walk(eng, body):
            base = 0
            for g in segs:
                n = g["w"].shape[1] // NB
                if n >= 4:
                    with eng.Fori(0, n // 2) as i:
                        for b in range(2):
                            body(g, i * 2 + (base + b), (base + b) % 2, i + (base + b) // 2, (i, b))
                else:
                    for c in range(n - n % 2):
                        body(g, base + c, (base + c) % 2, (base + c) // 2, (c // 2, c % 2))
                if n % 2:
                    body(g, base + n - 1, (base + n - 1) % 2, (base + n - 1) // 2, (n - 1,))
                base += n

        def columns(ap, at):
            if len(at) == 1:
                return rows(ap)[:, :, at[0] * NB:at[0] * NB + NB]
            n = ap.shape[1] // (2 * NB)
            return ap[:, 0:n * 2 * NB].rearrange("(k p) (i b n) -> i b p k n", p=P, b=2, n=NB)[at[0], at[1]]

        def channels(ap, at):
            if len(at) == 1:
                return rows(ap[at[0] * NB:at[0] * NB + NB, :])
            n = ap.shape[0] // (2 * NB)
            return ap[0:n * 2 * NB, :].rearrange("(i b c p) t -> i b p c t", b=2, c=4, p=P)[at[0], at[1]]

        @block.sync
        def _(sp):
            def load(g, j, buf, used, at):
                sp.wait_ge(split, j + 1)
                sp.dma_start(w_sb[:, :, :], columns(g["w"], at)).then_inc(w_in, 16)
                if g["kind"] == "conv":
                    sp.wait_ge(stored[buf], used * 16)
                    sp.dma_start(par[:, buf], channels(g["params"], at)).then_inc(par_in[buf], 16)
            walk(sp, load)

        @block.tensor
        def _(pe):
            pe.nop().then_inc(products, 8)

            def multiply(g, j, buf, used, at):
                pe.wait_ge(split, j + 2)
                for m in range(8):
                    pe.wait_ge(by_dve if m % 2 else by_act, j * 4 + (m // 2 + 1))
                    for k in range(kt):
                        if g["kind"] == "tok":
                            l = [a[:, k, m * P:m * P + P] for a in (a_hi, a_lo)]
                            r = [w[:, buf, k] for w in (w_hi, w_lo)]
                        else:
                            c, h = m // 2, m % 2
                            l = [w[:, buf, k, c * P:c * P + P] for w in (w_hi, w_lo)]
                            r = [a[:, k, h * 512:h * 512 + 512] for a in (a_hi, a_lo)]
                        mm = products3(pe, ps[:, m], l, r, k, kt)
                    mm.then_inc(products, 1)
            walk(pe, multiply)

        @block.scalar
        def _(act):
            act.nop().then_inc(by_act, 4)
            if has_conv:
                act.wait_ge(cleared, 1)

            def take(g, j, buf, used, at):
                if g["kind"] == "tok":
                    act.wait_ge(stored[buf], used * 16)
                    for m in range(0, 8, 2):
                        act.wait_ge(products, j * 8 + (m + 9))
                        act.activation(st[:, buf, m], ps[:, m], ACT.Copy).then_inc(by_act, 1)
                    act.wait_ge(by_act, j * 4 + 8)
                    act.wait_ge(by_dve, j * 4 + 8)
                    act.dma_start(columns(g["out"], at), st[:, buf]).then_inc(stored[buf], 16)
                    return

                def sigmoids(c):
                    act.wait_ge(summed, j * 4 + (c + 3))
                    act.wait_ge(gated, j * 4 + (c + 1))
                    act.activation(sig[:, c % 2], st[:, buf, 2 * c:2 * c + 2].rearrange("p a n -> p (a n)"),
                                   ACT.Sigmoid).then_inc(sigmoid, 1)
                for c in range(4):
                    act.wait_ge(products, j * 8 + (2 * c + 9))
                    act.wait_ge(summed, j * 4 + (c + 1))
                    act.activation(pad[:, c % 2, g["left"]:g["left"] + 512], ps[:, 2 * c], ACT.Copy).then_inc(by_act, 1)
                    if g["silu"] and c:
                        sigmoids(c - 1)
                if g["silu"]:
                    sigmoids(3)
                act.wait_ge(gated if g["silu"] else summed, j * 4 + 6)
                act.dma_start(channels(g["out"], at),
                              st[:, buf].rearrange("p (c h) n -> p c (h n)", h=2)).then_inc(stored[buf], 16)
            walk(act, take)
            for b in range(2):
                act.wait_ge(stored[b], 16 * ((n_all + 1 - b) // 2))

        @block.vector
        def _(v):
            v.nop().then_inc(by_dve, 4)
            if has_conv:
                v.nop().then_inc(summed, 2)
                v.nop().then_inc(gated, 2)
                v.memset(pad[:, :, :], 0.0).then_inc(cleared, 1)
                v.drain()

            def take(g, j, buf, used, at):
                if g["kind"] == "tok":
                    v.wait_ge(stored[buf], used * 16)
                    for m in range(1, 8, 2):
                        v.wait_ge(products, j * 8 + (m + 9))
                        v.tensor_copy(st[:, buf, m], ps[:, m]).then_inc(by_dve, 1)
                    return
                v.wait_ge(stored[buf], used * 16)
                v.wait_ge(par_in[buf], (used + 1) * 16)

                def gate(c):
                    v.wait_ge(sigmoid, j * 4 + (c + 1))
                    o = st[:, buf, 2 * c:2 * c + 2].rearrange("p a n -> p (a n)")
                    v.scalar_tensor_tensor(o, o, par[:, buf, c, taps + 1:taps + 2], sig[:, c % 2],
                                           ALU.mult, ALU.mult).then_inc(gated, 1)
                for c in range(4):
                    o = st[:, buf, 2 * c:2 * c + 2].rearrange("p a n -> p (a n)")
                    v.wait_ge(products, j * 8 + (2 * c + 10))
                    v.tensor_copy(pad[:, c % 2, g["left"] + 512:g["left"] + SEQ], ps[:, 2 * c + 1]).then_inc(by_dve, 1)
                    v.drain()
                    v.wait_ge(by_act, j * 4 + (c + 5))
                    v.tensor_scalar(o, pad[:, c % 2, 0:SEQ], par[:, buf, c, 0:1], par[:, buf, c, taps:taps + 1],
                                    ALU.mult, ALU.add)
                    for k in range(1, taps):
                        v.drain()
                        last = v.scalar_tensor_tensor(o, pad[:, c % 2, k:k + SEQ], par[:, buf, c, k:k + 1], o,
                                                      ALU.mult, ALU.add)
                    last.then_inc(summed, 1)
                    if g["silu"] and c:
                        gate(c - 1)
                if g["silu"]:
                    gate(3)
            walk(v, take)

        @block.gpsimd
        def _(pool):
            pool.nop().then_inc(split, 1)
            pool.memset(one[:, :], 1.0)
            pool.drain()

            def halve(g, j, buf, used, at):
                pool.wait_ge(w_in, j * 16 + 16)
                pool.wait_ge(products, j * 8)
                halves_on_pool(pool, w_sb[:, :, :], w_hi[:, buf], w_lo[:, buf], one, [P, kt, NB]).then_inc(split, 1)
            walk(pool, halve)
            if clear is not None:
                pool.memset(zero[:, :], 0.0)
                pool.drain()
                pool.dma_start(rows(clear)[:, 0:N_TILE], bc(zero[:, :].unsqueeze(1), [P, N_TILE, D])).then_inc(zeroed, 16)
                pool.wait_ge(zeroed, 16)


GATE_COLS = 2 * SSD_H + 3 * ML_H


def gates(nc, small, dt_bias, a_log, i_bias, f_bias, ident, gate_tab, m_rows):
    with Stage(nc, "gates") as s:
        dtb, al, ib, fb = (s.sb(n, [P, k]) for n, k in (("dtb", SSD_H), ("al", SSD_H), ("ib", ML_H), ("fb", ML_H)))
        n = SSD_H + ML_H
        x, u, w, d, ln, z, tab = (s.sb(k, [P, NT, n]) for k in ("x", "u", "w", "d", "ln", "z", "tab0"))
        tab = s.sb("tab", [P, NT, GATE_COLS])
        lfi = s.sb("lfi", [P, NT, 2 * ML_H])
        row = s.sb("row", [ML_H, 5, SEQ])
        m = s.sb("m", [ML_H, SEQ])
        one = s.sb("one", [ML_H, SEQ])
        ps_r, ps_t = s.ps("ps_r", [ML_H, 2, SEQ]), s.ps("ps_t", [P, NT, 3 * ML_H])
        b_in, pre, exped, w_ok, logd, a_exp, sp_ok, turned, rows_ok, back, tab_ok, m_out = (s.sem(k) for k in (
            "b_in", "pre", "exped", "w_ok", "logd", "a_exp", "sp_ok", "turned", "rows_ok", "back", "tab_ok", "m_out"))
        block = s.block()

        @block.sync
        def _(sp):
            for t, src in ((dtb, dt_bias), (al, a_log), (ib, i_bias), (fb, f_bias)):
                sp.dma_start(t[:, :], src.partition_broadcast(P)).then_inc(b_in, 16)
            sp.wait_ge(rows_ok, 1)
            sp.dma_start(m_rows, row[:, 4]).then_inc(m_out, 16)
            sp.wait_ge(tab_ok, 2)
            sp.dma_start(rows(gate_tab), tab[:, :, :]).then_inc(m_out, 16)
            sp.wait_ge(m_out, 32)

        @block.vector
        def _(v):
            v.wait_ge(b_in, 64)
            v.memset(one[:, :], 1.0)
            v.tensor_tensor(x[:, :, 0:SSD_H], small[:, :, 0:SSD_H], bc(dtb[:, :].unsqueeze(1), [P, NT, SSD_H]), ALU.add)
            v.tensor_tensor(lfi[:, :, ML_H:], small[:, :, SSD_H:SSD_H + ML_H],
                            bc(ib[:, :].unsqueeze(1), [P, NT, ML_H]), ALU.add)
            v.tensor_tensor(x[:, :, SSD_H:], small[:, :, SSD_H + ML_H:], bc(fb[:, :].unsqueeze(1), [P, NT, ML_H]), ALU.add)
            v.drain()
            v.tensor_scalar(x[:, :, SSD_H:], x[:, :, SSD_H:], -1.0, None, ALU.mult).then_inc(pre, 1)
            v.wait_ge(exped, 2)
            v.tensor_scalar(w[:, :, :], u[:, :, :], 1.0, None, ALU.add).then_inc(w_ok, 1)
            v.drain()
            v.tensor_scalar(d[:, :, :], w[:, :, :], -1.0, None, ALU.add)
            v.drain()
            v.tensor_scalar(z[:, :, :], d[:, :, :], 0.0, None, ALU.is_equal)
            v.drain()
            v.tensor_tensor(d[:, :, :], d[:, :, :], z[:, :, :], ALU.add)
            v.drain()
            v.reciprocal(d[:, :, :], d[:, :, :])
            v.drain()
            v.wait_ge(logd, 1)
            v.tensor_tensor(ln[:, :, :], ln[:, :, :], d[:, :, :], ALU.mult)
            v.drain()
            v.tensor_tensor(ln[:, :, :], ln[:, :, :], z[:, :, :], ALU.add)
            v.drain()
            v.tensor_tensor(ln[:, :, :], ln[:, :, :], u[:, :, :], ALU.mult)
            v.tensor_scalar(x[:, :, :], x[:, :, :], 0.0, None, ALU.max)
            v.drain()
            v.tensor_tensor(x[:, :, :], x[:, :, :], ln[:, :, :], ALU.add)
            v.drain()
            v.tensor_scalar(lfi[:, :, 0:ML_H], x[:, :, SSD_H:], -1.0, None, ALU.mult).then_inc(sp_ok, 1)
            v.tensor_copy(tab[:, :, 0:SSD_H], x[:, :, 0:SSD_H])
            v.wait_ge(a_exp, 1)
            v.tensor_tensor(tab[:, :, SSD_H:2 * SSD_H], x[:, :, 0:SSD_H], bc(al[:, :].unsqueeze(1), [P, NT, SSD_H]), ALU.mult)
            v.drain()
            v.tensor_scalar(tab[:, :, SSD_H:2 * SSD_H], tab[:, :, SSD_H:2 * SSD_H], -1.0, None, ALU.mult)
            v.wait_ge(turned, 1)
            v.tensor_copy(row[:, 0:2], ps_r[:, :, :])
            v.drain()
            v.tensor_tensor_scan(row[:, 2], one[:, :], row[:, 0], 0.0, ALU.mult, ALU.add)
            v.drain()
            v.tensor_tensor(row[:, 3], row[:, 1], row[:, 2], ALU.subtract)
            v.drain()
            v.tensor_tensor_scan(row[:, 4], row[:, 3], row[:, 3], -BIG, ALU.max, ALU.max)
            v.drain()
            v.tensor_tensor(m[:, :], row[:, 2], row[:, 4], ALU.add).then_inc(rows_ok, 1)
            v.wait_ge(back, 1)
            v.tensor_copy(tab[:, :, 2 * SSD_H:2 * SSD_H + 2 * ML_H], ps_t[:, :, 0:2 * ML_H]).then_inc(tab_ok, 1)

        @block.scalar
        def _(act):
            act.wait_ge(pre, 1)
            act.activation(u[:, :, :], x[:, :, :], ACT.Abs).then_inc(exped, 1)
            act.wait_ge(exped, 1)
            act.activation(u[:, :, :], u[:, :, :], ACT.Exp, scale=-1.0).then_inc(exped, 1)
            act.activation(al[:, :], al[:, :], ACT.Exp).then_inc(a_exp, 1)
            act.wait_ge(w_ok, 1)
            act.activation(ln[:, :, :], w[:, :, :], ACT.Ln).then_inc(logd, 1)
            act.wait_ge(tab_ok, 1)
            act.activation(tab[:, :, 2 * SSD_H + 2 * ML_H:], ps_t[:, :, 2 * ML_H:], ACT.Exp, scale=-1.0).then_inc(tab_ok, 1)

        @block.tensor
        def _(pe):
            pe.wait_ge(sp_ok, 1)
            for t in range(NT):
                pe.transpose(ps_r[:, 0, t * P:t * P + P], lfi[:, t, 0:ML_H], ident)
                mm = pe.transpose(ps_r[:, 1, t * P:t * P + P], lfi[:, t, ML_H:], ident)
            mm.then_inc(turned, 1)
            pe.wait_ge(rows_ok, 1)
            for t in range(NT):
                for q, src in enumerate((row[:, 3], row[:, 4], m[:, :])):
                    mm = pe.transpose(ps_t[:, t, q * ML_H:q * ML_H + ML_H], src[:, t * P:t * P + P],
                                      ident[0:ML_H, 0:ML_H])
            mm.then_inc(back, 1)


def ssd(nc, conv, z, gate_tab, d_skip, norm_w, ident, tri, ones, neg_mask, mix):
    H, G, HG = SSD_H, SSD_G, SSD_H // SSD_G
    W = SSD_W
    NX = W // P
    with Stage(nc, "ssd") as s:
        ch = s.sb("ch", [P, 2, NX + 2 * G, CHUNK])
        zt, gt = s.sb("zt", [P, 2, W]), s.sb("gt", [P, 2, 2 * H])
        dsk, nw = s.sb("dsk", [P, H]), s.sb("nw", [P, W])
        x, xdt, xdec, bt = s.sb("x", [P, W]), s.sb("xdt", [P, W]), s.sb("xdec", [P, W]), s.sb("bt", [P, G * SSD_N])
        acs, nadt = s.sb("acs", [P, 2 * H]), s.sb("nadt", [P, H])
        ea, dec, el = s.sb("ea", [P, H]), s.sb("dec", [P, H]), s.sb("el", [P, H])
        lm, mt = s.sb("lm", [P, 2, 4, CHUNK]), s.sb("mt", [P, 2, 4, CHUNK])
        state = s.sb("state", [P, W])
        y, y2, out, st2, rs = s.sb("y", [P, W]), s.sb("y2", [P, W]), s.sb("out", [P, 2, W]), s.sb("st2", [P, G]), s.sb("rs", [P, G])
        p_x = s.ps("p_x", [P, W])
        p_b = s.ps("p_b", [P, 512])
        p_s = s.ps("p_s", [P, G, 4, 64])
        p_d = [s.ps(f"p_d{k}", [P, 4, CHUNK]) for k in range(2)]
        p_y = s.ps("p_y", [P, W])
        cb = p_s[:, :, :, :].rearrange("p g a b -> p (g a b)")[:, 0:G * CHUNK].rearrange("p (g l) -> p g l", g=G)
        c_in, loaded = s.sem("c_in"), [s.sem(f"loaded{b}") for b in range(2)]
        stored = [s.sem(f"stored{b}") for b in range(2)]
        (turned, x_taken, nadt_ok, acs_ok, exps, dec_pre, xdec_ok, diff, lmat, mts, y_done, inter, y_taken, st_new,
         st_done, zsig, ssum, root, n_ready, out_ok, cb_used) = (s.sem(k) for k in (
             "turned", "x_taken", "nadt_ok", "acs_ok", "exps", "dec_pre", "xdec_ok", "diff", "lmat", "mts", "y_done",
             "inter", "y_taken", "st_new", "st_done", "zsig", "ssum", "root", "n_ready", "out_ok", "cb_used"))
        block = s.block()

        def chunks(eng, body):
            with eng.Fori(0, NCH // 2) as i:
                for b in range(2):
                    body(i * 2 + b, b, i)

        def h3(ap, n=H):
            return ap.rearrange("p (h q) -> p h q", h=n)

        @block.sync
        def _(sp):
            sp.dma_start(dsk[:, :], d_skip.partition_broadcast(P)).then_inc(c_in, 16)
            sp.dma_start(nw[:, :], norm_w.partition_broadcast(P)).then_inc(c_in, 16)

            def load(j, b, i):
                sp.wait_ge(out_ok, j)
                sp.dma_start(ch[:, b], conv[0:XBC, :].rearrange("(c p) (i b t) -> i b p c t", p=P, b=2, t=CHUNK)[i, b]
                             ).then_inc(loaded[b], 16)
                sp.dma_start(zt[:, b], z.rearrange("(i b p) n -> i b p n", b=2, p=P)[i, b]).then_inc(loaded[b], 16)
                sp.dma_start(gt[:, b], gate_tab[:, 0:2 * H].rearrange("(i b p) n -> i b p n", b=2, p=P)[i, b]
                             ).then_inc(loaded[b], 16)
            chunks(sp, load)

        @block.tensor
        def _(pe):
            def step(j, b, i):
                pe.wait_ge(loaded[b], i * 48 + 48)
                pe.wait_ge(y_taken, j)
                for c in range(NX):
                    pe.transpose(p_x[:, c * P:c * P + P], ch[:, b, c], ident)
                pe.wait_ge(x_taken, j)
                for g in range(G):
                    pe.transpose(p_b[:, g * SSD_N:g * SSD_N + SSD_N], ch[:, b, NX + g], ident)
                pe.matmul(p_b[:, 256:256 + H], tri, gt[:, b, H:2 * H], start=True, stop=True)
                pe.matmul(p_b[:, 256 + H:256 + 2 * H], ones, gt[:, b, H:2 * H], start=True, stop=True).then_inc(turned, 1)
                pe.wait_ge(mts, j * 4)
                for g in range(G):
                    pe.matmul(cb[:, g], ch[:, b, NX + g], ch[:, b, NX + G + g], start=True, stop=True)
                pe.wait_ge(nadt_ok, j + 1)
                pe.wait_ge(st_done, j)
                for q in range(4):
                    if q >= 2:
                        pe.wait_ge(lmat, j * 4 + (q - 1))
                    for k in range(4):
                        h = 4 * q + k
                        o = p_d[q % 2][:, k]
                        pe.matmul(o, bc(gt[:, b, H + h:H + h + 1], [P, CHUNK]), tri, start=True, stop=False)
                        pe.matmul(o, tri, bc(nadt[:, h:h + 1], [P, CHUNK]), start=False, stop=False)
                        mm = pe.matmul(o, ident, neg_mask, start=False, stop=True)
                    mm.then_inc(diff, 1)
                pe.wait_ge(x_taken, j + 1)
                pe.wait_ge(st_new, j + 1)
                for g in range(G):
                    mm = pe.matmul(p_x[:, g * 512:g * 512 + 512], ch[:, b, NX + G + g], state[:, g * 512:g * 512 + 512],
                                   start=True, stop=True)
                mm.then_inc(inter, 1)
                for q in range(4):
                    pe.wait_ge(mts, j * 4 + (q + 1))
                    for k in range(4):
                        h = 4 * q + k
                        mm = pe.matmul(p_y[:, h * 64:h * 64 + 64], mt[:, q % 2, k], xdt[:, h * 64:h * 64 + 64],
                                       start=True, stop=True)
                    mm.then_inc(y_done, 1)
                pe.wait_ge(xdec_ok, j + 1)
                pe.wait_ge(lmat, j * 4 + 4)
                for g in range(G):
                    mm = pe.matmul(p_d[g][:, :, :].rearrange("p a b -> p (a b)"), bt[:, g * SSD_N:g * SSD_N + SSD_N],
                                   xdec[:, g * 512:g * 512 + 512], start=True, stop=True)
                mm.then_inc(st_done, 1)
            chunks(pe, step)

        @block.scalar
        def _(act):
            def step(j, b, i):
                act.wait_ge(acs_ok, j + 1)
                act.activation(ea[:, :], acs[:, 0:H], ACT.Exp)
                act.activation(el[:, :], acs[:, H:2 * H], ACT.Exp)
                act.activation(dec[:, :], dec[:, :], ACT.Exp).then_inc(exps, 1)
                for q in range(4):
                    act.wait_ge(diff, j * 4 + (q + 1))
                    act.wait_ge(mts, j * 4 + q)
                    act.activation(lm[:, q % 2], p_d[q % 2][:, :, :], ACT.Exp).then_inc(lmat, 1)
                act.wait_ge(loaded[b], i * 48 + 48)
                act.wait_ge(stored[b], i * 16)
                act.activation(out[:, b], zt[:, b], ACT.Sigmoid).then_inc(zsig, 1)
                act.wait_ge(n_ready, j + 1)
                act.activation(rs[:, :], st2[:, :], ACT.Sqrt).then_inc(root, 1)
            chunks(act, step)

        @block.vector
        def _(v):
            v.memset(state[:, :], 0.0).then_inc(st_new, 1)
            v.wait_ge(c_in, 32)
            v.nop().then_inc(out_ok, 1)

            def step(j, b, i):
                v.wait_ge(loaded[b], i * 48 + 48)
                v.tensor_scalar(nadt[:, :], gt[:, b, H:2 * H], -1.0, None, ALU.mult).then_inc(nadt_ok, 1)
                v.wait_ge(turned, j + 1)
                v.tensor_copy(acs[:, :], p_b[:, 256:256 + 2 * H])
                v.tensor_copy(bt[:, :], p_b[:, 0:G * SSD_N])
                v.drain()
                v.tensor_tensor(dec[:, :], acs[:, H:2 * H], acs[:, 0:H], ALU.subtract).then_inc(acs_ok, 1)
                v.tensor_copy(x[:, :], p_x[:, :]).then_inc(x_taken, 1)
                v.drain()
                v.tensor_tensor(h3(xdt[:, :]), h3(x[:, :]), bc(gt[:, b, 0:H].unsqueeze(2), [P, H, 64]), ALU.mult)
                v.drain()
                v.wait_ge(exps, j + 1)
                v.tensor_tensor(h3(xdec[:, :]), h3(xdt[:, :]), bc(dec[:, :].unsqueeze(2), [P, H, 64]),
                                ALU.mult).then_inc(xdec_ok, 1)
                for q in range(4):
                    v.wait_ge(lmat, j * 4 + (q + 1))
                    if q >= 2:
                        v.wait_ge(y_done, j * 4 + (q - 1))
                    v.tensor_tensor(mt[:, q % 2], lm[:, q % 2], bc(cb[:, q // 2].unsqueeze(1), [P, 4, CHUNK]),
                                    ALU.mult).then_inc(mts, 1)
                    if q == 0:
                        v.tensor_tensor(h3(y2[:, :]), h3(x[:, :]), bc(dsk[:, :].unsqueeze(2), [P, H, 64]), ALU.mult)
                        v.wait_ge(inter, j + 1)
                        v.tensor_tensor(h3(y[:, :]), h3(p_x[:, :]), bc(ea[:, :].unsqueeze(2), [P, H, 64]),
                                        ALU.mult).then_inc(y_taken, 1)
                        v.drain()
                        v.tensor_tensor(y2[:, :], y2[:, :], y[:, :], ALU.add)
                v.tensor_tensor(h3(state[:, :]), h3(state[:, :]), bc(el[:, :].unsqueeze(2), [P, H, 64]), ALU.mult)
                v.drain()
                v.wait_ge(st_done, j + 1)
                for g in range(G):
                    last = v.tensor_tensor(state[:, g * 512:g * 512 + 512], state[:, g * 512:g * 512 + 512],
                                           p_d[g][:, :, :].rearrange("p a b -> p (a b)"), ALU.add)
                last.then_inc(st_new, 1)
                v.wait_ge(y_done, j * 4 + 4)
                v.tensor_tensor(y2[:, :], y2[:, :], p_y[:, :], ALU.add)
                v.wait_ge(zsig, j + 1)
                v.tensor_tensor(y[:, :], out[:, b], zt[:, b], ALU.mult)
                v.drain()
                v.tensor_tensor(y2[:, :], y2[:, :], y[:, :], ALU.mult)
                v.drain()
                for g in range(G):
                    v.scalar_tensor_tensor(y[:, g * 512:g * 512 + 512], y2[:, g * 512:g * 512 + 512], 1.0,
                                           y2[:, g * 512:g * 512 + 512], ALU.mult, ALU.mult, accum_out=st2[:, g:g + 1])
                v.drain()
                v.tensor_scalar(st2[:, :], st2[:, :], 1.0 / 512, EPS, ALU.mult, ALU.add).then_inc(n_ready, 1)
                v.wait_ge(root, j + 1)
                v.reciprocal(st2[:, :], rs[:, :])
                v.drain()
                for g in range(G):
                    last = v.scalar_tensor_tensor(out[:, b, g * 512:g * 512 + 512], y2[:, g * 512:g * 512 + 512],
                                                  st2[:, g:g + 1], nw[:, g * 512:g * 512 + 512], ALU.mult, ALU.mult)
                last.then_inc(out_ok, 1)
            chunks(v, step)

        @block.gpsimd
        def _(pool):
            def store(j, b, i):
                pool.wait_ge(out_ok, j + 2)
                pool.dma_start(mix[:, 0:W].rearrange("(i b p) n -> i b p n", b=2, p=P)[i, b], out[:, b]
                               ).then_inc(stored[b], 16)
            chunks(pool, store)
            for b in range(2):
                pool.wait_ge(stored[b], 16 * (NCH // 2))


def mlstm(nc, conv, vo, gate_tab, m_rows, norm_w, ident, ones, neg_mask, mix):
    H, DH, HH = ML_H, ML_D, 4
    W = ML_W
    with Stage(nc, "ml") as s:
        qk = s.sb("qk", [P, 2, 2 * H, CHUNK])
        vt = s.sb("vt", [P, 2, 2 * W])
        gt, mrow = s.sb("gt", [P, 2, 3 * H]), s.sb("mrow", [P, 2, H, CHUNK])
        nw, m_prev = s.sb("nw", [P, W]), s.sb("m_prev", [P, 2, H])
        kw = s.sb("kw", [P, 2, HH, DH])
        arg, wt, ws = s.sb("arg", [P, 2, HH, CHUNK]), s.sb("wt", [P, 2, HH, CHUNK]), s.sb("ws", [P, 2, HH, CHUNK])
        wc, inter, cs = s.sb("wc", [P, H]), s.sb("inter", [P, H]), s.sb("cs", [P, H])
        mem, nrm = s.sb("mem", [P, W]), s.sb("nrm", [P, H])
        num, den, rden = s.sb("num", [P, 2, W]), s.sb("den", [P, H]), s.sb("rden", [P, H])
        osig, sq = s.sb("osig", [P, W]), s.sb("sq", [P, W])
        mean, var, rs = s.sb("mean", [P, H]), s.sb("var", [P, H]), s.sb("rs", [P, H])
        p_s = s.ps("p_s", [P, HH, CHUNK])
        p_k = s.ps("p_k", [P, HH, DH])
        p_n = [s.ps(f"p_n{k}", [P, HH, DH]) for k in range(2)]
        p_i = s.ps("p_i", [P, HH, DH])
        p_m = s.ps("p_m", [P, HH, DH])
        p_d = s.ps("p_d", [P, 512])
        p_u = s.ps("p_u", [P, 512])
        nw_in, loaded = s.sem("nw_in"), [s.sem(f"loaded{b}") for b in range(2)]
        stored = [s.sem(f"stored{b}") for b in range(2)]
        (scores, kturned, pre, wts, arg_ok, w_ok, ws_ok, kw_ok, nums, inters, upd, num_taken, upd_taken, osig_ok,
         chunk_ok, root, scores_used, mem_ok, sq_ok, sq_in) = (s.sem(k) for k in (
             "scores", "kturned", "pre", "wts", "arg_ok", "w_ok", "ws_ok", "kw_ok", "nums", "inters", "upd",
             "num_taken", "upd_taken", "osig_ok", "chunk_ok", "root", "scores_used", "mem_ok", "sq_ok", "sq_in"))
        block = s.block()

        def chunks(eng, body):
            with eng.Fori(0, NCH // 2) as i:
                for b in range(2):
                    body(i * 2 + b, b, i)

        def h3(ap, n=H):
            return ap.rearrange("p (h q) -> p h q", h=n)

        @block.sync
        def _(sp):
            sp.dma_start(nw[:, :], norm_w.partition_broadcast(P)).then_inc(nw_in, 16)

            def load(j, b, i):
                sp.wait_ge(chunk_ok, j)
                sp.dma_start(qk[:, b], conv[XBC:, :].rearrange("(c p) (i b t) -> i b p c t", p=P, b=2, t=CHUNK)[i, b]
                             ).then_inc(loaded[b], 16)
                sp.dma_start(vt[:, b], vo.rearrange("(i b p) n -> i b p n", b=2, p=P)[i, b]).then_inc(loaded[b], 16)
                sp.dma_start(gt[:, b], gate_tab[:, 2 * SSD_H:].rearrange("(i b p) n -> i b p n", b=2, p=P)[i, b]
                             ).then_inc(loaded[b], 16)
                sp.dma_start(mrow[:, b], m_rows.rearrange("h (i b t) -> i b h t", b=2, t=CHUNK)[i, b]
                             .partition_broadcast(P)).then_inc(loaded[b], 16)
            chunks(sp, load)

        @block.tensor
        def _(pe):
            def step(j, b, i):
                pe.wait_ge(loaded[b], i * 64 + 64)
                for f in range(2):
                    n = j * 2 + f
                    pe.wait_ge(ws_ok, n)
                    for k in range(HH):
                        h = HH * f + k
                        mm = pe.matmul(p_s[:, k], qk[:, b, H + h], qk[:, b, h], start=True, stop=True)
                    mm.then_inc(scores, 1)
                    pe.wait_ge(kw_ok, n)
                    for k in range(HH):
                        mm = pe.transpose(p_k[:, k], qk[:, b, H + HH * f + k], ident)
                    mm.then_inc(kturned, 1)
                    pe.wait_ge(num_taken, n)
                    pe.wait_ge(mem_ok, j * 2 + (f + 1))
                    for k in range(HH):
                        h = HH * f + k
                        pe.matmul(p_i[:, k], qk[:, b, h], mem[:, h * DH:h * DH + DH], start=True, stop=True)
                        mm = pe.matmul(p_d[:, H + h:H + h + 1], qk[:, b, h], nrm[:, h:h + 1], start=True, stop=True)
                    mm.then_inc(inters, 1)
                    pe.wait_ge(ws_ok, n + 1)
                    for k in range(HH):
                        h = HH * f + k
                        pe.matmul(p_n[f][:, k], ws[:, f, k], vt[:, b, h * DH:h * DH + DH], start=True, stop=True)
                        mm = pe.matmul(p_d[:, h:h + 1], ws[:, f, k], ones[:, 0:1], start=True, stop=True)
                    mm.then_inc(nums, 1)
                    pe.wait_ge(kw_ok, n + 1)
                    for k in range(HH):
                        h = HH * f + k
                        pe.matmul(p_m[:, k], kw[:, f, k], vt[:, b, h * DH:h * DH + DH], start=True, stop=True)
                        mm = pe.matmul(p_u[:, h:h + 1], kw[:, f, k], ones[:, 0:1], start=True, stop=True)
                    mm.then_inc(upd, 1)
            chunks(pe, step)

        @block.scalar
        def _(act):
            def step(j, b, i):
                act.wait_ge(pre, j + 1)
                for t in (wc, inter, cs):
                    last = act.activation(t[:, :], t[:, :], ACT.Exp)
                last.then_inc(wts, 1)
                for f in range(2):
                    act.wait_ge(arg_ok, j * 2 + (f + 1))
                    for k in range(HH):
                        h = HH * f + k
                        last = act.activation(wt[:, f, k], arg[:, f, k], ACT.Exp, scale=-1.0, bias=gt[:, b, h:h + 1])
                    last.then_inc(w_ok, 1)
                act.wait_ge(chunk_ok, j + 1)
                act.activation(osig[:, :], vt[:, b, W:], ACT.Sigmoid).then_inc(osig_ok, 1)
                act.wait_ge(sq_in, j + 1)
                act.activation(sq[:, :], num[:, b], ACT.Square).then_inc(sq_ok, 1)
                act.wait_ge(root, j * 2 + 1)
                act.activation(rs[:, :], var[:, :], ACT.Sqrt).then_inc(root, 1)
            chunks(act, step)

        @block.vector
        def _(v):
            v.memset(mem[:, :], 0.0)
            v.memset(nrm[:, :], 0.0)
            v.memset(m_prev[:, 1], -BIG)
            v.drain()
            v.nop().then_inc(mem_ok, 2)
            v.nop().then_inc(chunk_ok, 1)
            v.wait_ge(nw_in, 16)

            def step(j, b, i):
                m_end = mrow[:, b, :, CHUNK - 1]
                v.drain()
                v.wait_ge(loaded[b], i * 64 + 64)
                v.tensor_tensor(wc[:, :], gt[:, b, 0:H], m_end, ALU.subtract)
                v.tensor_tensor(inter[:, :], m_prev[:, 1 - b], gt[:, b, H:2 * H], ALU.subtract)
                v.tensor_tensor(cs[:, :], m_prev[:, 1 - b], m_end, ALU.subtract).then_inc(pre, 1)
                v.tensor_copy(m_prev[:, b], m_end)
                for f in range(2):
                    n = j * 2 + f
                    v.tensor_tensor(arg[:, f], mrow[:, b, HH * f:HH * f + HH],
                                    bc(neg_mask.unsqueeze(1), [P, HH, CHUNK]), ALU.subtract).then_inc(arg_ok, 1)
                for f in range(2):
                    n = j * 2 + f
                    v.wait_ge(w_ok, n + 1)
                    v.wait_ge(scores, n + 1)
                    v.tensor_tensor(ws[:, f], wt[:, f], p_s[:, :, :], ALU.mult).then_inc(ws_ok, 1)
                    v.wait_ge(wts, j + 1)
                    v.wait_ge(kturned, n + 1)
                    v.tensor_tensor(kw[:, f], p_k[:, :, :], bc(wc[:, HH * f:HH * f + HH].unsqueeze(2), [P, HH, DH]),
                                    ALU.mult).then_inc(kw_ok, 1)
                    if f == 0:
                        v.wait_ge(stored[b], i * 16)
                    v.wait_ge(inters, n + 1)
                    nf = num[:, b, 512 * f:512 * f + 512]
                    v.tensor_tensor(h3(nf, HH), p_i[:, :, :], bc(inter[:, HH * f:HH * f + HH].unsqueeze(2), [P, HH, DH]),
                                    ALU.mult)
                    v.wait_ge(nums, n + 1)
                    v.tensor_tensor(den[:, HH * f:HH * f + HH], p_d[:, H + HH * f:H + HH * f + HH],
                                    inter[:, HH * f:HH * f + HH], ALU.mult)
                    v.drain()
                    v.tensor_tensor(den[:, HH * f:HH * f + HH], den[:, HH * f:HH * f + HH], p_d[:, HH * f:HH * f + HH], ALU.add)
                    v.tensor_tensor(h3(nf, HH), h3(nf, HH), p_n[f][:, :, :], ALU.add).then_inc(num_taken, 1)
                    mf, rf = mem[:, 512 * f:512 * f + 512], nrm[:, HH * f:HH * f + HH]
                    v.tensor_tensor(h3(mf, HH), h3(mf, HH), bc(cs[:, HH * f:HH * f + HH].unsqueeze(2), [P, HH, DH]), ALU.mult)
                    v.tensor_tensor(rf, rf, cs[:, HH * f:HH * f + HH], ALU.mult)
                    v.drain()
                    v.wait_ge(upd, n + 1)
                    v.tensor_tensor(h3(mf, HH), h3(mf, HH), p_m[:, :, :], ALU.add)
                    v.tensor_tensor(rf, rf, p_u[:, HH * f:HH * f + HH], ALU.add).then_inc(mem_ok, 1)
                v.drain()
                v.scalar_tensor_tensor(rden[:, :], den[:, :], -1.0, den[:, :], ALU.mult, ALU.max)
                v.drain()
                v.tensor_tensor(rden[:, :], rden[:, :], gt[:, b, 2 * H:3 * H], ALU.max)
                v.drain()
                v.reciprocal(rden[:, :], rden[:, :])
                v.drain()
                v.tensor_tensor(h3(num[:, b]), h3(num[:, b]), bc(rden[:, :].unsqueeze(2), [P, H, DH]), ALU.mult)
                v.drain()
                v.tensor_reduce(mean[:, :], h3(num[:, b]), AXX, ALU.add)
                v.drain()
                v.tensor_scalar(mean[:, :], mean[:, :], 1.0 / DH, None, ALU.mult)
                v.drain()
                v.tensor_tensor(h3(num[:, b]), h3(num[:, b]), bc(mean[:, :].unsqueeze(2), [P, H, DH]),
                                ALU.subtract).then_inc(sq_in, 1)
                v.wait_ge(sq_ok, j + 1)
                v.tensor_reduce(var[:, :], h3(sq[:, :]), AXX, ALU.add)
                v.drain()
                v.tensor_scalar(var[:, :], var[:, :], 1.0 / DH, EPS, ALU.mult, ALU.add).then_inc(root, 1)
                v.wait_ge(root, j * 2 + 2)
                v.reciprocal(rs[:, :], rs[:, :])
                v.drain()
                v.tensor_tensor(h3(num[:, b]), h3(num[:, b]), bc(rs[:, :].unsqueeze(2), [P, H, DH]), ALU.mult)
                v.drain()
                v.tensor_tensor(num[:, b], num[:, b], nw[:, :], ALU.mult)
                v.drain()
                v.wait_ge(osig_ok, j + 1)
                v.tensor_tensor(num[:, b], num[:, b], osig[:, :], ALU.mult).then_inc(chunk_ok, 1)
            chunks(v, step)

        @block.gpsimd
        def _(pool):
            def store(j, b, i):
                pool.wait_ge(chunk_ok, j + 2)
                pool.dma_start(mix[:, SSD_W:].rearrange("(i b p) n -> i b p n", b=2, p=P)[i, b], num[:, b]
                               ).then_inc(stored[b], 16)
            chunks(pool, store)
            for b in range(2):
                pool.wait_ge(stored[b], 16 * (NCH // 2))


def transpose_in(nc, name, src, dst_t, ident, col0=0):
    kt = dst_t.shape[1]
    per = 8
    with Stage(nc, name) as s:
        xt, ps = s.sb("xt", [P, NT, per * P]), s.ps("ps", [P, 8, 512])
        x_in, turned, by_act, by_dve = (s.sem(n) for n in ("x_in", "turned", "by_act", "by_dve"))
        block = s.block()
        n_load = (kt + per - 1) // per
        widths = [min(per, kt - per * a) for a in range(n_load)]
        steps = [(a, k, h) for a in range(n_load) for k in range(widths[a]) for h in range(2)]
        first = [sum(2 * w for w in widths[:a]) for a in range(n_load + 1)]

        @block.sync
        def _(sp):
            for a in range(n_load):
                if a:
                    sp.wait_ge(turned, first[a])
                sp.dma_start(xt[:, :, 0:widths[a] * P],
                             rows(src)[:, :, col0 + a * per * P:col0 + a * per * P + widths[a] * P]).then_inc(x_in, 16)

        @block.tensor
        def _(pe):
            for j, (a, k, h) in enumerate(steps):
                pe.wait_ge(x_in, 16 * (a + 1))
                if j >= 8:
                    pe.wait_ge(by_dve if j % 2 else by_act, (j - 8) // 2 + 1)
                for q in range(4):
                    mm = pe.transpose(ps[:, j % 8, q * P:q * P + P], xt[:, 4 * h + q, k * P:k * P + P], ident)
                mm.then_inc(turned, 1)

        def take(eng, odd, done):
            for j, (a, k, h) in enumerate(steps):
                if j % 2 == odd:
                    eng.wait_ge(turned, j + 1)
                    o = dst_t[:, a * per + k, h * 512:h * 512 + 512]
                    if odd:
                        eng.tensor_copy(o, ps[:, j % 8]).then_inc(done, 1)
                    else:
                        eng.activation(o, ps[:, j % 8], ACT.Copy).then_inc(done, 1)

        @block.scalar
        def _(act):
            take(act, 0, by_act)

        @block.vector
        def _(v):
            take(v, 1, by_dve)


def residual_norm(nc, name, x, w, ident, hT=None, alpha=1.0, add=None, bias=None, eps=EPS, sum_out=None,
                  y_out=None, also=()):
    layer = bias is not None
    with Stage(nc, name) as s:
        r, y, sq = s.sb("r", [P, NT, D]), s.sb("y", [P, NT, D]), s.sb("sq", [P, D])
        wr, br = s.sb("wr", [P, D]), s.sb("br", [P, D])
        mean, nmean, ssq, var, root, rstd = (s.sb(n, [P, NT]) for n in ("mean", "nmean", "ssq", "var", "root", "rstd"))
        ps = s.ps("ps", [P, 4, D // P, P])
        x_in = [s.sem(f"x_in{t}") for t in range(NT)]
        w_in, added, sums, mean_ok, squares, var_ok, root_ok, scaled, weighted, normed, turned, taken, by_act, out = (
            s.sem(n) for n in ("w_in", "added", "sums", "mean_ok", "squares", "var_ok", "root_ok", "scaled", "weighted", "normed",
                               "turned", "taken", "by_act", "out"))
        also_in = s.sem("also_in")
        block = s.block()

        def turns(steps):
            for n in range(NT + max(lag for lag, _ in steps)):
                for lag, step in steps:
                    if 0 <= n - lag < NT:
                        step(n - lag)

        @block.sync
        def _(sp):
            sp.dma_start(wr[:, :], w.partition_broadcast(P)).then_inc(w_in, 16)
            if layer:
                sp.dma_start(br[:, :], bias.partition_broadcast(P)).then_inc(w_in, 16)
            for t in range(NT):
                sp.dma_start(r[:, t], x[t * P:(t + 1) * P, :]).then_inc(x_in[t], 16)
                if add is not None:
                    sp.dma_start(y[:, t], add[t * P:(t + 1) * P, :]).then_inc(x_in[t], 16)
            n_out = 0
            if y_out is not None:
                for t in range(NT):
                    if sum_out is not None:
                        sp.wait_ge(added, t + 1)
                        sp.dma_start(sum_out[t * P:(t + 1) * P, :], r[:, t]).then_inc(out, 16)
                        n_out += 16
                    sp.wait_ge(normed, t + 1)
                    sp.dma_start(y_out[t * P:(t + 1) * P, :], y[:, t]).then_inc(out, 16)
                    n_out += 16
            if n_out:
                sp.wait_ge(out, n_out)

        @block.scalar
        def _(act):
            def total(t):
                act.wait_ge(added, t + 1)
                act.activation(sq[:, :], r[:, t], ACT.Identity, accum_out=mean[:, t:t + 1]).then_inc(sums, 1)
                act.wait_ge(sums, t + 1)

            def square(t):
                if layer:
                    act.wait_ge(mean_ok, t + 1)
                    act.activation(sq[:, :], r[:, t], ACT.Square, bias=nmean[:, t:t + 1],
                                   accum_out=ssq[:, t:t + 1]).then_inc(squares, 1)
                else:
                    act.wait_ge(added, t + 1)
                    act.activation(sq[:, :], r[:, t], ACT.Square, accum_out=ssq[:, t:t + 1]).then_inc(squares, 1)
                act.wait_ge(squares, t + 1)

            def take_root(t):
                act.wait_ge(var_ok, t + 1)
                act.activation(root[:, t:t + 1], var[:, t:t + 1], ACT.Sqrt).then_inc(root_ok, 1)

            def high(t):
                act.wait_ge(turned, t + 1)
                act.activation(hT[0][:, :, t * P:t * P + P], ps[:, t % 4], ACT.Copy).then_inc(by_act, 1)
            first = 1 if layer else 0
            turns(([(0, total)] if layer else []) + [(first, square), (first + 1, take_root)]
                  + ([(2 * first + 3, high)] if hT is not None else []))

        @block.vector
        def _(v):
            def residual(t):
                v.wait_ge(x_in[t], 16 if add is None else 32)
                if add is not None:
                    v.scalar_tensor_tensor(r[:, t], r[:, t], float(alpha), y[:, t], ALU.mult, ALU.add).then_inc(added, 1)
                else:
                    v.nop().then_inc(added, 1)

            def centre(t):
                v.wait_ge(sums, t + 1)
                v.tensor_scalar(nmean[:, t:t + 1], mean[:, t:t + 1], -1.0 / D, None, ALU.mult).then_inc(mean_ok, 1)

            def variance(t):
                v.wait_ge(squares, t + 1)
                v.tensor_scalar(var[:, t:t + 1], ssq[:, t:t + 1], 1.0 / D, float(eps), ALU.mult, ALU.add).then_inc(var_ok, 1)

            def scale(t):
                v.wait_ge(root_ok, t + 1)
                v.reciprocal(rstd[:, t:t + 1], root[:, t:t + 1])
                v.drain()
                if layer:
                    v.tensor_scalar(y[:, t], r[:, t], nmean[:, t:t + 1], rstd[:, t:t + 1], ALU.add, ALU.mult).then_inc(scaled, 1)
                else:
                    if t == 0:
                        v.wait_ge(w_in, 16)
                    v.scalar_tensor_tensor(y[:, t], r[:, t], rstd[:, t:t + 1], wr[:, :], ALU.mult, ALU.mult).then_inc(normed, 1)

            def shift(t):
                v.wait_ge(weighted, t + 1)
                v.tensor_tensor(y[:, t], y[:, t], br[:, :], ALU.add).then_inc(normed, 1)

            def low(t):
                v.wait_ge(by_act, t + 1)
                v.tensor_tensor(hT[1][:, :, t * P:t * P + P], ps[:, t % 4], hT[0][:, :, t * P:t * P + P],
                                ALU.subtract).then_inc(taken, 1)
            first = 1 if layer else 0
            turns([(0, residual)] + ([(1, centre)] if layer else []) + [(first + 1, variance), (first + 2, scale)]
                  + ([(first + 4, shift)] if layer else []) + ([(2 * first + 4, low)] if hT is not None else []))

        @block.gpsimd
        def _(pool):
            for dst, src in also:
                pool.dma_start(dst, src).then_inc(also_in, 16)
            if layer:
                pool.wait_ge(w_in, 32)
                for t in range(NT):
                    pool.wait_ge(scaled, t + 1)
                    pool.tensor_tensor(y[:, t], y[:, t], wr[:, :], ALU.mult).then_inc(weighted, 1)
            if also:
                pool.wait_ge(also_in, 16 * len(also))

        @block.tensor
        def _(pe):
            if hT is not None:
                for t in range(NT):
                    pe.wait_ge(normed, t + 1)
                    if t >= 4:
                        pe.wait_ge(taken, t - 3)
                    for k in range(D // P):
                        mm = pe.transpose(ps[:, t % 4, k], y[:, t, k * P:k * P + P], ident)
                    mm.then_inc(turned, 1)


def route(nc, logits, bias_g, bias_e, tri_strict, ones, iotas, h2, xs, gate2, slots, tile_exp, ident):
    E, NG, PG = N_EXP, N_GROUP, PER_GROUP
    with Stage(nc, "route") as s:
        bg, be, io = s.sb("bg", [P, NG]), s.sb("be", [P, E]), s.sb("io", [P, 64])
        h2t = s.sb("h2t", [P, NT, D])
        lg, le, mg = s.sb("lg", [P, NT, 8]), s.sb("le", [P, NT, E]), s.sb("mg", [P, NT, 8])
        ig, ie = s.sb("ig", [P, NT, 8], U32), s.sb("ie", [P, NT, 8], U32)
        fg, fe, me = s.sb("fg", [P, NT, 1]), s.sb("fe", [P, NT, 2]), s.sb("me", [P, NT, 8])
        oh, eg, pg = s.sb("oh", [P, NT, NG]), s.sb("eg", [P, NT, NG]), s.sb("pg", [P, NT])
        one_hot, both = s.sb("one_hot", [P, 2, NT, E]), s.sb("both", [P, NT, E])
        df = s.sb("df", [P, NT, 1])
        cnt, nt_, end, one, big = (s.sb("cnt", [P, E]), s.sb("nt", [P, E]), s.sb("end", [P, E]), s.sb("one", [P, E]),
                                   s.sb("big", [P, N_LIST, E]))
        rank, pick, slot_f, te = (s.sb("rank", [P, NT, E]), s.sb("pick", [P, 2, NT, E]), s.sb("slot_f", [P, 2, NT]),
                                  s.sb("te", [P, N_LIST + 1]))
        p_r, p_c = s.ps("p_r", [P, NT, E]), s.ps("p_c", [P, 512])
        c_in, h_in, pre, exps, hots, ranks, slot_ok, moved = (s.sem(n) for n in (
            "c_in", "h_in", "pre", "exps", "hots", "ranks", "slot_ok", "moved"))
        block = s.block()

        @block.sync
        def _(sp):
            sp.dma_start(bg[:, :], bias_g.partition_broadcast(P)).then_inc(c_in, 16)
            sp.dma_start(be[:, :], bias_e.partition_broadcast(P)).then_inc(c_in, 16)
            sp.dma_start(io[:, :], iotas.partition_broadcast(P)).then_inc(c_in, 16)
            sp.dma_start(h2t[:, :, :], rows(h2)).then_inc(h_in, 16)

        @block.vector
        def _(v):
            v.memset(lg[:, :, :], -BIG)
            v.memset(one[:, :], 1.0)
            v.drain()
            v.wait_ge(c_in, 48)
            v.tensor_tensor(lg[:, :, 0:NG], logits[:, :, 0:NG], bc(bg[:, :].unsqueeze(1), [P, NT, NG]), ALU.add)
            v.tensor_tensor(le[:, :, :], logits[:, :, NG:], bc(be[:, :].unsqueeze(1), [P, NT, E]), ALU.add)
            v.drain()
            for t in range(NT):
                v.max(mg[:, t], lg[:, t])
            v.drain()
            for t in range(NT):
                v.max_index(ig[:, t], mg[:, t], lg[:, t])
            v.drain()
            v.tensor_copy(fg[:, :, :], ig[:, :, 0:1])
            v.tensor_tensor(eg[:, :, :], lg[:, :, 0:NG], bc(mg[:, :, 0:1], [P, NT, NG]), ALU.subtract)
            v.drain()
            v.tensor_tensor(oh[:, :, :], bc(io[:, 0:NG].unsqueeze(1), [P, NT, NG]), bc(fg[:, :, :], [P, NT, NG]), ALU.is_equal)
            v.drain()
            v.tensor_scalar(oh[:, :, :], oh[:, :, :], -1.0, BIG, ALU.add, ALU.mult)
            v.drain()
            for t in range(NT):
                v.tensor_tensor(le[:, t].rearrange("p (g e) -> p g e", g=NG), le[:, t].rearrange("p (g e) -> p g e", g=NG),
                                bc(oh[:, t].unsqueeze(2), [P, NG, PG]), ALU.add)
            v.drain()
            for t in range(NT):
                v.max(me[:, t], le[:, t])
            v.drain()
            for t in range(NT):
                v.max_index(ie[:, t], me[:, t], le[:, t])
            v.tensor_tensor(df[:, :, :], me[:, :, 1:2], me[:, :, 0:1], ALU.subtract).then_inc(pre, 1)
            v.drain()
            v.tensor_copy(fe[:, :, :], ie[:, :, 0:2])
            v.drain()
            for k in range(2):
                v.tensor_tensor(one_hot[:, k], bc(io[:, 0:E].unsqueeze(1), [P, NT, E]), bc(fe[:, :, k:k + 1], [P, NT, E]),
                                ALU.is_equal)
            v.drain()
            v.tensor_tensor(both[:, :, :], one_hot[:, 0], one_hot[:, 1], ALU.add).then_inc(hots, 1)
            v.wait_ge(exps, 1)
            v.tensor_reduce(pg[:, :], eg[:, :, :], AXX, ALU.add)
            v.tensor_scalar(gate2[:, :, 0:1], df[:, :, :], 1.0, None, ALU.add)
            v.drain()
            v.tensor_tensor(gate2[:, :, 0:1], gate2[:, :, 0:1], pg[:, :].unsqueeze(2), ALU.mult)
            v.drain()
            v.reciprocal(gate2[:, :, 0:1], gate2[:, :, 0:1])
            v.drain()
            v.tensor_tensor(gate2[:, :, 1:2], gate2[:, :, 0:1], df[:, :, :], ALU.mult)
            v.wait_ge(ranks, 1)
            v.tensor_copy(cnt[:, :], p_c[:, 0:E])
            v.tensor_copy(rank[:, :, :], p_r[:, :, :])
            v.drain()
            v.tensor_scalar(nt_[:, :], cnt[:, :], 0.0, None, ALU.is_gt)
            for r in range(1, NT):
                v.drain()
                v.scalar_tensor_tensor(nt_[:, :], cnt[:, :], float(P * r), nt_[:, :], ALU.is_gt, ALU.add)
            v.drain()
            v.tensor_tensor_scan(end[:, :], one[:, :], nt_[:, :], 0.0, ALU.mult, ALU.add)
            v.drain()
            v.tensor_tensor(big[:, :, :], bc(end[:, :].unsqueeze(1), [P, N_LIST, E]),
                            bc(io[:, 0:N_LIST].unsqueeze(2), [P, N_LIST, E]), ALU.is_le)
            v.tensor_tensor(cnt[:, :], end[:, :], nt_[:, :], ALU.subtract)
            v.tensor_copy(te[:, N_LIST:], end[:, E - 1:E])
            v.drain()
            v.tensor_reduce(te[:, 0:N_LIST], big[:, :, :], AXX, ALU.add)
            v.tensor_scalar(cnt[:, :], cnt[:, :], float(P), None, ALU.mult)
            v.drain()
            v.tensor_scalar(tile_exp[:, 0:N_LIST], te[:, 0:N_LIST], float(E - 1), None, ALU.min)
            v.tensor_copy(tile_exp[:, N_LIST:], te[:, N_LIST:])
            v.tensor_tensor(rank[:, :, :], rank[:, :, :], bc(cnt[:, :].unsqueeze(1), [P, NT, E]), ALU.add)
            v.drain()
            for k in range(2):
                v.tensor_tensor(pick[:, k], one_hot[:, k], rank[:, :, :], ALU.mult)
            v.drain()
            for k in range(2):
                v.tensor_reduce(slot_f[:, k], pick[:, k], AXX, ALU.add)
            v.drain()
            for k in range(2):
                last = v.tensor_copy(slots[:, k], slot_f[:, k])
            last.then_inc(slot_ok, 1)

        @block.scalar
        def _(act):
            act.wait_ge(pre, 1)
            act.activation(df[:, :, :], df[:, :, :], ACT.Exp)
            act.activation(eg[:, :, :], eg[:, :, :], ACT.Exp).then_inc(exps, 1)

        @block.tensor
        def _(pe):
            pe.wait_ge(hots, 1)
            for t in range(NT):
                for e in range(t):
                    pe.matmul(p_r[:, t], ones, both[:, e], start=(e == 0), stop=False)
                pe.matmul(p_r[:, t], tri_strict, both[:, t], start=(t == 0), stop=True)
            for t in range(NT):
                mm = pe.matmul(p_c[:, 0:E], ones, both[:, t], start=(t == 0), stop=(t == NT - 1))
            mm.then_inc(ranks, 1)

        @block.gpsimd
        def _(pool):
            pool.wait_ge(slot_ok, 1)
            pool.wait_ge(h_in, 16)
            for t in range(NT):
                for k in range(2):
                    pool.indirect_dma_start(xs[:, :], bass.IndirectOffsetOnAxis(ap=slots[:, k, t:t + 1], axis=0),
                                            h2t[:, t], None).then_inc(moved, 16)
            pool.wait_ge(moved, 16 * 2 * NT)


def experts(nc, xs, ys, w_gate, w_up, w_down, tile_exp, ident):
    KD, KF = D // P, D_EXP // P
    with Stage(nc, "moe") as s:
        x = s.sb("x", [P, 2, D])
        wg, wu, wd = s.sb("wg", [P, KD, D_EXP]), s.sb("wu", [P, KD, D_EXP]), s.sb("wd", [P, KF, D])
        wg_hi, wg_lo, wu_hi, wu_lo = (s.sb(n, [P, KD, D_EXP], HALF) for n in ("wg_hi", "wg_lo", "wu_hi", "wu_lo"))
        wd_hi, wd_lo = (s.sb(n, [P, KF, D], HALF) for n in ("wd_hi", "wd_lo"))
        xT_hi, xT_lo, aT_hi, aT_lo = (s.sb("xT_hi", [P, KD, P], HALF), s.sb("xT_lo", [P, KD, P], HALF),
                                      s.sb("aT_hi", [P, KF, P], HALF), s.sb("aT_lo", [P, KF, P], HALF))
        a, sg, y = s.sb("a", [P, D_EXP]), s.sb("sg", [P, D_EXP]), s.sb("y", [P, 2, D])
        p_x, p_g, p_u, p_a, p_y = (s.ps("p_x", [P, KD, P]), s.ps("p_g", [P, D_EXP]), s.ps("p_u", [P, D_EXP]),
                                   s.ps("p_a", [P, KF, P]), s.ps("p_y", [P, D]))
        x_in, stored = ([s.sem(f"{n}{b}") for b in range(2)] for n in ("x_in", "stored"))
        g_in, u_in, d_in = (s.sem(n) for n in ("g_in", "u_in", "d_in"))
        turned, xt_hi, xt_lo, g_hi, g_lo, u_hi, u_lo, d_hi, d_lo, a_turned, at_hi, at_lo = (s.sem(n) for n in (
            "turned", "xt_hi", "xt_lo", "g_hi", "g_lo", "u_hi", "u_lo", "d_hi", "d_lo", "a_turned", "at_hi", "at_lo"))
        gated, upped, downed, sig, act_ok, y_act, y_dve = (s.sem(n) for n in (
            "gated", "upped", "downed", "sig", "act_ok", "y_act", "y_dve"))
        block = s.block()

        def steps(eng, first, body, skipped=None):
            n_used = eng.value_load(tile_exp[0:1, N_LIST:N_LIST + 1], min_val=1, max_val=N_TILE)

            def run(j, b, k):
                with eng.If(n_used >= j):
                    body(j, b, k, n_used)
                if skipped:
                    with eng.Else():
                        skipped(j, b)
            for j in range(first):
                body(j, j % 2, j // 2, n_used)
            b0 = first % 2
            n = N_TILE + 1 - first
            with eng.Fori(0, n // 2) as i:
                run(i * 2 + first, b0, i + first // 2)
                run(i * 2 + (first + 1), 1 - b0, i + (first + 1) // 2)
            if n % 2:
                run(N_TILE, N_TILE % 2, N_TILE // 2)

        @block.sync
        def _(sp):
            def expert(j):
                return sp.value_load(tile_exp[0:1, bass.ds(j, 1)], min_val=0, max_val=N_EXP - 1)

            def weights(sem, w, src, e, j, n_used):
                sp.dma_start(w[:, :, :], src.rearrange("e (k p) n -> e p k n", p=P)[e], cond=(n_used > j)).then_inc(sem, 16)

            def ahead(j, b, k, n_used):
                first = isinstance(j, int) and j == 0
                e, e1 = expert(j), expert(j + 1)
                if not first:
                    sp.wait_ge(turned, j)
                sp.dma_start(x[:, 1 - b], xs.rearrange("(j p) n -> j p n", p=P)[j + 1],
                             cond=(n_used > j + 1)).then_inc(x_in[1 - b], 16)
                sp.wait_ge(g_lo, j + 1)
                weights(g_in, wg, w_gate, e1, j + 1, n_used)
                sp.wait_ge(u_lo, j + 1)
                weights(u_in, wu, w_up, e1, j + 1, n_used)
                if not first:
                    sp.wait_ge(d_lo, j)
                weights(d_in, wd, w_down, e, j, n_used)

            def step(j, b, k, n_used):
                if isinstance(j, int) and j == 0:
                    sp.dma_start(x[:, 0], xs[0:P, :]).then_inc(x_in[0], 16)
                    e = expert(0)
                    weights(g_in, wg, w_gate, e, 0, n_used)
                    weights(u_in, wu, w_up, e, 0, n_used)
                ahead(j, b, k, n_used)
            steps(sp, 1, step)

        @block.tensor
        def _(pe):
            pe.nop().then_inc(y_act, 1)
            pe.nop().then_inc(y_dve, 1)

            def turn_rows(b):
                for k in range(KD):
                    mm = pe.transpose(p_x[:, k], x[:, b, k * P:k * P + P], ident)
                mm.then_inc(turned, 1)
            pe.wait_ge(x_in[0], 16)
            turn_rows(0)

            def step(j, b, k2, n_used):
                first = isinstance(j, int) and j == 0
                pe.wait_ge(xt_lo, j + 1)
                pe.wait_ge(g_lo, j + 1)
                if not first:
                    pe.wait_ge(sig, j)
                for k in range(KD):
                    mm = products3(pe, p_g[:, :], (xT_hi[:, k], xT_lo[:, k]), (wg_hi[:, k], wg_lo[:, k]), k, KD)
                mm.then_inc(gated, 1)
                if not first:
                    pe.wait_ge(act_ok, j)
                    for k in range(KF):
                        mm = pe.transpose(p_a[:, k], a[:, k * P:k * P + P], ident)
                    mm.then_inc(a_turned, 1)
                pe.wait_ge(u_lo, j + 1)
                for k in range(KD):
                    mm = products3(pe, p_u[:, :], (xT_hi[:, k], xT_lo[:, k]), (wu_hi[:, k], wu_lo[:, k]), k, KD)
                mm.then_inc(upped, 1)
                pe.wait_ge(x_in[1 - b], (k2 + b) * 16 + 16)
                turn_rows(1 - b)
                if not first:
                    pe.wait_ge(at_lo, j)
                    pe.wait_ge(d_lo, j)
                    pe.wait_ge(y_act, j)
                    pe.wait_ge(y_dve, j)
                    for h in range(2):
                        n = slice(h * 512, h * 512 + 512)
                        for k in range(KF):
                            mm = products3(pe, p_y[:, n], (aT_hi[:, k], aT_lo[:, k]), (wd_hi[:, k, n], wd_lo[:, k, n]), k, KF)
                    mm.then_inc(downed, 1)
            steps(pe, 1, step)

        @block.scalar
        def _(act):
            for b in range(2):
                act.nop().then_inc(stored[b], 16)
            act.wait_ge(g_in, 16)
            act.activation(wg_hi[:, :, :], wg[:, :, :], ACT.Copy).then_inc(g_hi, 1)
            act.wait_ge(turned, 1)
            act.activation(xT_hi[:, :, :], p_x[:, :, :], ACT.Copy).then_inc(xt_hi, 1)
            act.wait_ge(u_in, 16)
            act.activation(wu_hi[:, :, :], wu[:, :, :], ACT.Copy).then_inc(u_hi, 1)

            def step(j, b, k, n_used):
                first = isinstance(j, int) and j == 0
                act.wait_ge(gated, j + 1)
                if not first:
                    act.wait_ge(act_ok, j)
                act.activation(sg[:, :], p_g[:, :], ACT.Silu).then_inc(sig, 1)
                if not first:
                    act.wait_ge(a_turned, j)
                    act.activation(aT_hi[:, :, :], p_a[:, :, :], ACT.Copy).then_inc(at_hi, 1)
                act.wait_ge(g_in, j * 16 + 32)
                act.activation(wg_hi[:, :, :], wg[:, :, :], ACT.Copy).then_inc(g_hi, 1)
                act.wait_ge(turned, j + 2)
                act.activation(xT_hi[:, :, :], p_x[:, :, :], ACT.Copy).then_inc(xt_hi, 1)
                act.wait_ge(u_in, j * 16 + 32)
                act.activation(wu_hi[:, :, :], wu[:, :, :], ACT.Copy).then_inc(u_hi, 1)
                if not first:
                    act.wait_ge(downed, j)
                    act.wait_ge(stored[1 - b], (k + b) * 16)
                    act.activation(y[:, 1 - b, 0:512], p_y[:, 0:512], ACT.Copy).then_inc(y_act, 1)
                act.wait_ge(d_in, j * 16 + 16)
                act.activation(wd_hi[:, :, :], wd[:, :, :], ACT.Copy).then_inc(d_hi, 1)
                if not first:
                    act.wait_ge(y_act, j + 1)
                    act.wait_ge(y_dve, j + 1)
                    act.dma_start(ys.rearrange("(j p) n -> j p n", p=P)[j - 1], y[:, 1 - b]).then_inc(stored[1 - b], 16)

            def skipped(j, b):
                act.dma_start(ys.rearrange("(j p) n -> j p n", p=P)[j - 1], y[:, 1 - b]).then_inc(stored[1 - b], 16)
            steps(act, 1, step, skipped)
            for b in range(2):
                act.wait_ge(stored[b], 16 + 16 * ((N_TILE + 1 - b) // 2))

        @block.vector
        def _(v):
            v.wait_ge(xt_hi, 1)
            v.tensor_tensor(xT_lo[:, :, :], p_x[:, :, :], xT_hi[:, :, :], ALU.subtract).then_inc(xt_lo, 1)

            def step(j, b, k, n_used):
                first = isinstance(j, int) and j == 0
                if not first:
                    v.wait_ge(at_hi, j)
                    v.tensor_tensor(aT_lo[:, :, :], p_a[:, :, :], aT_hi[:, :, :], ALU.subtract).then_inc(at_lo, 1)
                v.wait_ge(sig, j + 1)
                v.wait_ge(upped, j + 1)
                v.tensor_tensor(a[:, :], sg[:, :], p_u[:, :], ALU.mult).then_inc(act_ok, 1)
                v.wait_ge(xt_hi, j + 2)
                v.tensor_tensor(xT_lo[:, :, :], p_x[:, :, :], xT_hi[:, :, :], ALU.subtract).then_inc(xt_lo, 1)
                if not first:
                    v.wait_ge(downed, j)
                    v.wait_ge(stored[1 - b], (k + b) * 16)
                    v.tensor_copy(y[:, 1 - b, 512:], p_y[:, 512:]).then_inc(y_dve, 1)
                v.wait_ge(d_hi, j + 1)
                v.tensor_tensor(wd_lo[:, :, :], wd[:, :, :], wd_hi[:, :, :], ALU.subtract).then_inc(d_lo, 1)
            steps(v, 1, step)

        @block.gpsimd
        def _(pool):
            def low(sem_hi, sem_lo, w, hi, lo, n):
                pool.wait_ge(sem_hi, n)
                pool.tensor_tensor(lo[:, :, :], w[:, :, :], hi[:, :, :], ALU.subtract).then_inc(sem_lo, 1)
            low(g_hi, g_lo, wg, wg_hi, wg_lo, 1)
            low(u_hi, u_lo, wu, wu_hi, wu_lo, 1)

            def step(j, b, k, n_used):
                low(g_hi, g_lo, wg, wg_hi, wg_lo, j + 2)
                low(u_hi, u_lo, wu, wu_hi, wu_lo, j + 2)
            steps(pool, 1, step)


def combine(nc, ys, gate2, slots, out):
    with Stage(nc, "comb") as s:
        a = s.sb("a", [P, NT, 2, D])
        got, mixed, stored = [s.sem(f"got{t}") for t in range(NT)], s.sem("mixed"), s.sem("stored")
        block = s.block()

        @block.gpsimd
        def _(pool):
            for t in range(NT):
                for k in range(2):
                    pool.indirect_dma_start(a[:, t, k], None, ys[:, :],
                                            bass.IndirectOffsetOnAxis(ap=slots[:, k, t:t + 1], axis=0)).then_inc(got[t], 16)

        @block.vector
        def _(v):
            for t in range(NT):
                v.wait_ge(got[t], 32)
                v.tensor_scalar(a[:, t, 0], a[:, t, 0], gate2[:, t, 0:1], None, ALU.mult)
                v.drain()
                v.scalar_tensor_tensor(a[:, t, 0], a[:, t, 1], gate2[:, t, 1:2], a[:, t, 0], ALU.mult,
                                       ALU.add).then_inc(mixed, 1)

        @block.sync
        def _(sp):
            for t in range(NT):
                sp.wait_ge(mixed, t + 1)
                sp.dma_start(out[t * P:(t + 1) * P, :], a[:, t, 0]).then_inc(stored, 16)
            sp.wait_ge(stored, 16 * NT)


def conv_params(nc, hy_w, hy_b, mu, par):
    nh, nr, n = HY_COLS // P, RW_COLS // P, par.shape[0] // P
    with Stage(nc, "par") as s:
        t = s.sb("t", [P, n, 5])
        hw, hb, m = s.sb("hw", [P, 3, nh]), s.sb("hb", [P, nh]), s.sb("m", [P, nr])
        got, made, out = s.sem("got"), s.sem("made"), s.sem("out")
        block = s.block()

        @block.sync
        def _(sp):
            for k in range(3):
                sp.dma_start(hw[:, k], hy_w[k].rearrange("(c p) -> p c", p=P), allow_slow_non_contiguous=True).then_inc(got, 16)
            sp.dma_start(hb[:, :], hy_b.rearrange("(c p) -> p c", p=P), allow_slow_non_contiguous=True).then_inc(got, 16)
            sp.dma_start(m[:, :], mu.rearrange("(c p) -> p c", p=P), allow_slow_non_contiguous=True).then_inc(got, 16)
            sp.wait_ge(made, 1)
            sp.dma_start(rows(par), t[:, :, :]).then_inc(out, 16)
            sp.wait_ge(out, 16)

        @block.vector
        def _(v):
            v.memset(t[:, :, :], 0.0)
            v.drain()
            v.wait_ge(got, 80)
            for k in range(3):
                v.tensor_copy(t[:, 0:nh, k:k + 1], hw[:, k].unsqueeze(2))
            v.tensor_copy(t[:, 0:nh, 3:4], hb[:, :].unsqueeze(2))
            for k in (0, 2):
                v.tensor_scalar(t[:, nh:nh + nr, k:k + 1], m[:, :].unsqueeze(2), 0.5, None, ALU.mult)
            v.tensor_scalar(t[:, nh:nh + nr, 1:2], m[:, :].unsqueeze(2), -1.0, 1.0, ALU.mult, ALU.add)
            v.drain()
            v.nop().then_inc(made, 1)


def hyena_filters(nc, feats_t, window, w1, b1, w2, b2, w3, b3, w4, sin_freq, sums):
    NH, EMB = 64, 33
    TWO_PI = 2.0 * np.pi
    C1 = 6.28125
    C2 = float(np.float32(TWO_PI - C1))
    C3 = float(TWO_PI - C1 - C2)
    MAGIC = 12582912.0
    with Stage(nc, "filt") as s:
        ft = s.sb("ft", [EMB, SEQ])
        wa, wb, wc, wd = s.sb("wa", [EMB, NH]), s.sb("wb", [NH, NH]), s.sb("wc", [NH, NH]), s.sb("wd", [NH, 4 * HY_W])
        bb, sf = s.sb("bb", [NH, 3]), s.sb("sf", [NH, 3])
        h, k, m = s.sb("h", [NH, SEQ]), s.sb("k", [NH, SEQ]), s.sb("m", [NH, SEQ])
        win = s.sb("win", [P, NT, HY_W])
        fl, o = s.sb("fl", [P, 2, 4, HY_W]), s.sb("o", [P, 2, 4, HY_W])
        ps, pf = s.ps("ps", [P, SEQ]), s.ps("pf", [P, 4, HY_W])
        got, product, arg, sine, taken, filt, windowed, made, stored = (s.sem(n) for n in (
            "got", "product", "arg", "sine", "taken", "filt", "windowed", "made", "stored"))
        block = s.block()

        @block.sync
        def _(sp):
            sp.dma_start(ft[:, :], feats_t).then_inc(got, 16)
            for t, src in ((wa, w1), (wb, w2), (wc, w3), (wd, w4)):
                sp.dma_start(t[:, :], src).then_inc(got, 16)
            for q, src in enumerate((b1, b2, b3)):
                sp.dma_start(bb[:, q:q + 1], src.rearrange("(p a) -> p a", a=1)).then_inc(got, 16)
                sp.dma_start(sf[:, q:q + 1], sin_freq[q].rearrange("(p a) -> p a", a=1)).then_inc(got, 16)
            sp.dma_start(win[:, :, :], rows(window)).then_inc(got, 16)
            for t in range(NT):
                sp.wait_ge(made, t + 1)
                sp.dma_start(sums.rearrange("o s (t p) n -> t p (o s) n", p=P)[t], o[:, t % 2]).then_inc(stored, 16)
                sp.wait_ge(stored, 16 * (t + 1))
                sp.nop().then_inc(taken, 1)

        @block.tensor
        def _(pe):
            pe.wait_ge(got, 12 * 16)
            for q, w in enumerate((wa, wb, wc)):
                if q:
                    pe.wait_ge(sine, q)
                src = ft if q == 0 else h
                for c in range(2):
                    mm = pe.matmul(ps[0:NH, c * 512:c * 512 + 512], w[:, :], src[:, c * 512:c * 512 + 512], start=True, stop=True)
                mm.then_inc(product, 1)
            pe.wait_ge(sine, 3)
            for t in range(NT):
                if t:
                    pe.wait_ge(windowed, t)
                for c in range(4):
                    mm = pe.matmul(pf[:, c], h[:, t * P:t * P + P], wd[:, c * 512:c * 512 + 512], start=True, stop=True)
                mm.then_inc(filt, 1)

        @block.scalar
        def _(act):
            for q in range(3):
                act.wait_ge(arg, q + 1)
                act.activation(h[:, :], m[:, :], ACT.Sin).then_inc(sine, 1)

        @block.vector
        def _(v):
            for q in range(3):
                v.wait_ge(product, q + 1)
                v.tensor_scalar(m[:, :], ps[0:NH, :], bb[:, q:q + 1], sf[:, q:q + 1], ALU.add, ALU.mult)
                v.drain()
                v.tensor_scalar(k[:, :], m[:, :], 1.0 / TWO_PI, None, ALU.mult)
                v.drain()
                v.tensor_scalar(k[:, :], k[:, :], MAGIC, None, ALU.add)
                v.drain()
                v.tensor_scalar(k[:, :], k[:, :], -MAGIC, None, ALU.add)
                for c in (C1, C2, C3):
                    v.drain()
                    last = v.scalar_tensor_tensor(m[:, :], k[:, :], -c, m[:, :], ALU.mult, ALU.add)
                v.drain()
                v.tensor_scalar(m[:, :], m[:, :], 3.1415925, -3.1415925, ALU.min, ALU.max).then_inc(arg, 1)
            for t in range(NT):
                v.wait_ge(filt, t + 1)
                v.tensor_tensor(fl[:, t % 2], pf[:, :, :], bc(win[:, t].unsqueeze(1), [P, 4, HY_W]), ALU.mult).then_inc(windowed, 1)
                v.drain()
                if t >= 2:
                    v.wait_ge(taken, t - 1)
                f4 = fl[:, t % 2].rearrange("p (o d) n -> p o d n", d=2)
                o4 = o[:, t % 2].rearrange("p (o d) n -> p o d n", d=2)
                v.tensor_tensor(o4[:, :, 0], f4[:, :, 0], f4[:, :, 1], ALU.add)
                v.tensor_tensor(o4[:, :, 1], f4[:, :, 0], f4[:, :, 1], ALU.subtract)
                v.drain()
                v.nop().then_inc(made, 1)


def filter_spectrum(nc, name, sums, table, spec):
    with Stage(nc, name) as s:
        f, tb, one = s.sb("f", [P, 2, NT, HY_W]), s.sb("tb", [P, 2, NT, P]), s.sb("one", [P, 1])
        f_hi, f_lo = (s.sb(n, [P, 2, NT, HY_W], HALF) for n in ("f_hi", "f_lo"))
        tb_hi, tb_lo = (s.sb(n, [P, 2, 2, NT, P], HALF) for n in ("tb_hi", "tb_lo"))
        o, top = s.sb("o", [P, 2, 2, HY_W]), s.sb("top", [1, HY_W])
        ps = s.ps("ps", [P, 4, HY_W])
        pn = s.ps("pn", [2, HY_W])
        f_in, t_in, done, nyq, taken, stored, high, low, split = (
            s.sem("f_in"), s.sem("t_in"), s.sem("done"), s.sem("nyq"), s.sem("taken"),
            [s.sem(f"stored{b}") for b in range(2)], s.sem("high"), s.sem("low"), s.sem("split"))
        block = s.block()

        @block.sync
        def _(sp):
            for k in range(2):
                sp.dma_start(f[:, k], rows(sums[k])).then_inc(f_in, 16)
            with sp.Fori(0, NT // 2) as i:
                for b in range(2):
                    sp.wait_ge(split, i * 2 + (b + 1))
                    sp.dma_start(tb[:, :, :, :], table.rearrange("(i b) s p k n -> i b p s k n", b=2)[i, b]).then_inc(t_in, 16)

        @block.gpsimd
        def _(pool):
            pool.nop().then_inc(split, 1)
            pool.memset(one[:, :], 1.0)
            pool.drain()
            with pool.Fori(0, NT // 2) as i:
                for b in range(2):
                    pool.wait_ge(t_in, (i * 2 + b) * 16 + 16)
                    pool.wait_ge(done, i * 2 + b)
                    halves_on_pool(pool, tb[:, :, :, :], tb_hi[:, b], tb_lo[:, b], one, [P, 2, NT, P]).then_inc(split, 1)

        @block.tensor
        def _(pe):
            pe.nop().then_inc(done, 1)
            pe.wait_ge(split, 2)
            for k in range(NT):
                pe.wait_ge(low, k + 1)
                mm = products3(pe, pn[:, :], [w[:, 0, 1, k, 0:2] for w in (tb_hi, tb_lo)],
                               [w[:, 0, k] for w in (f_hi, f_lo)], k, NT)
            mm.then_inc(nyq, 1)
            pe.wait_ge(low, 2 * NT)
            with pe.Fori(0, NT // 2) as i:
                for b in range(2):
                    pe.wait_ge(split, i * 2 + (b + 2))
                    pe.wait_ge(taken, i * 2 + (b + 1))
                    for c in range(2):
                        for k in range(NT):
                            mm = products3(pe, ps[:, 2 * b + c], [w[:, b, c, k] for w in (tb_hi, tb_lo)],
                                           [w[:, c, k] for w in (f_hi, f_lo)], k, NT)
                    mm.then_inc(done, 1)

        @block.vector
        def _(v):
            v.nop().then_inc(taken, 2)
            v.wait_ge(f_in, 32)
            for c in range(2):
                for k in range(NT):
                    v.wait_ge(high, c * NT + k + 1)
                    v.tensor_tensor(f_lo[:, c, k], f[:, c, k], f_hi[:, c, k], ALU.subtract).then_inc(low, 1)
            v.wait_ge(nyq, 1)
            v.tensor_copy(top[:, :], pn[0:1, :])
            v.drain()
            with v.Fori(0, NT // 2) as i:
                for b in range(2):
                    v.wait_ge(stored[b], i * 16)
                    v.wait_ge(done, i * 2 + (b + 2))
                    v.tensor_copy(o[:, b], ps[:, 2 * b:2 * b + 2]).then_inc(taken, 1)

        @block.scalar
        def _(act):
            act.wait_ge(f_in, 32)
            for c in range(2):
                for k in range(NT):
                    act.activation(f_hi[:, c, k], f[:, c, k], ACT.Copy).then_inc(high, 1)
            with act.Fori(0, NT // 2) as i:
                for b in range(2):
                    act.wait_ge(taken, i * 2 + (b + 3))
                    act.dma_start(spec.rearrange("(i b) s p n -> i b p s n", b=2)[i, b], o[:, b]).then_inc(stored[b], 16)
            for b in range(2):
                act.wait_ge(stored[b], NT // 2 * 16)
            act.dma_start(spec[0, 1, 0:1, :], top[:, :]).then_inc(stored[0], 16)
            act.wait_ge(stored[0], NT // 2 * 16 + 16)


def long_conv(nc, name, z, gate, spec, skip, table, inv_table, out):
    with Stage(nc, name) as s:
        tb, one = s.sb("tb", [P, 2 * NT, P]), s.sb("one", [P, 1])
        tb_hi, tb_lo = (s.sb(n, [P, 2, 2 * NT, P], HALF) for n in ("tb_hi", "tb_lo"))
        z_hi, z_lo = (s.sb(n, [P, NT, HY_W], HALF) for n in ("z_hi", "z_lo"))
        y_hi, y_lo = (s.sb(n, [P, 2, NT, HY_W], HALF) for n in ("y_hi", "y_lo"))
        sp_ = s.sb("sp", [P, 2, 2, HY_W])
        tmp, sk = s.sb("tmp", [P, 4, HY_W]), s.sb("sk", [P, HY_W])
        ps, pi = s.ps("ps", [P, 4, HY_W]), s.ps("pi", [P, 2, HY_W])
        t_in, s_in = s.sem("t_in"), [s.sem(f"s_in{b}") for b in range(2)]
        k_in, done, used, taken, split, low = (s.sem(n) for n in ("k_in", "done", "used", "taken", "split", "low"))
        block = s.block()

        @block.sync
        def _(sp):
            sp.dma_start(sk[:, :], skip.partition_broadcast(P)).then_inc(k_in, 16)
            with sp.Fori(0, NT // 2) as i:
                for b in range(2):
                    sp.wait_ge(split, i * 2 + (b + 1))
                    sp.dma_start(tb[:, :, :].rearrange("p (s k) n -> p s k n", s=2),
                                 table.rearrange("(i b) s p k n -> i b p s k n", b=2)[i, b]).then_inc(t_in, 16)
                    sp.wait_ge(used, i * 2 + b)
                    sp.dma_start(sp_[:, b], spec.rearrange("(i b) s p n -> i b p s n", b=2)[i, b]).then_inc(s_in[b], 16)
            with sp.Fori(0, NT // 2) as i:
                for b in range(2):
                    sp.wait_ge(split, i * 2 + (NT + b + 1))
                    sp.dma_start(tb[:, :, :], inv_table.rearrange("(i b) p k n -> i b p k n", b=2)[i, b]).then_inc(t_in, 16)

        @block.gpsimd
        def _(pool):
            pool.nop().then_inc(split, 1)
            pool.memset(one[:, :], 1.0)
            pool.drain()
            with pool.Fori(0, NT) as i:
                for b in range(2):
                    pool.wait_ge(t_in, (i * 2 + b) * 16 + 16)
                    pool.wait_ge(done, i * 2 + b)
                    halves_on_pool(pool, tb[:, :, :], tb_hi[:, b], tb_lo[:, b], one, [P, 2 * NT, P]).then_inc(split, 1)

        @block.tensor
        def _(pe):
            pe.nop().then_inc(done, 1)
            pe.wait_ge(low, NT)
            with pe.Fori(0, NT // 2) as i:
                for b in range(2):
                    pe.wait_ge(split, i * 2 + (b + 2))
                    pe.wait_ge(used, i * 2 + b)
                    for c in range(2):
                        for k in range(NT):
                            mm = products3(pe, ps[:, 2 * b + c], [w[:, b, c * NT + k] for w in (tb_hi, tb_lo)],
                                           [w[:, k] for w in (z_hi, z_lo)], k, NT)
                    mm.then_inc(done, 1)
            pe.wait_ge(used, NT + 1)
            with pe.Fori(0, NT // 2) as i:
                for b in range(2):
                    pe.wait_ge(split, i * 2 + (NT + b + 2))
                    pe.wait_ge(taken, i * 2 + b)
                    for k in range(2 * NT):
                        mm = products3(pe, pi[:, b], [w[:, b, k] for w in (tb_hi, tb_lo)],
                                       [w[:, k // NT, k % NT] for w in (y_hi, y_lo)], k, 2 * NT)
                    mm.then_inc(done, 1)

        @block.vector
        def _(v):
            v.nop().then_inc(used, 1)
            v.nop().then_inc(taken, 1)
            v.wait_ge(k_in, 16)
            for k in range(NT):
                v.tensor_copy(z_hi[:, k], z[:, k])
                v.drain()
                v.tensor_tensor(z_lo[:, k], z[:, k], z_hi[:, k], ALU.subtract).then_inc(low, 1)

            pairs_hi, pairs_lo = (w[:, :, :, :].rearrange("p s (i b) n -> p s i b n", b=2) for w in (y_hi, y_lo))

            def product(i, b, first=False):
                v.wait_ge(done, i * 2 + (b + 2))
                v.wait_ge(s_in[b], i * 16 + 16)
                cz, sz, chh, sh = ps[:, 2 * b], ps[:, 2 * b + 1], sp_[:, b, 0], sp_[:, b, 1]
                v.tensor_tensor(tmp[:, 0], cz, chh, ALU.mult)
                v.tensor_tensor(tmp[:, 1], sz, sh, ALU.mult)
                v.tensor_tensor(tmp[:, 2], cz, sh, ALU.mult)
                v.tensor_tensor(tmp[:, 3], sz, chh, ALU.mult)
                v.drain()
                v.tensor_tensor(tmp[:, 2], tmp[:, 2], tmp[:, 3], ALU.add)
                if first:
                    v.drain()
                    v.tensor_copy(tmp[0:1, 2], tmp[0:1, 1])
                    v.drain()
                    v.memset(tmp[0:1, 1], 0.0)
                    v.drain()
                v.tensor_tensor(tmp[:, 0], tmp[:, 0], tmp[:, 1], ALU.subtract)
                v.drain()
                both = tmp[:, :].rearrange("p (s a) n -> p s a n", a=2)[:, :, 0]
                v.tensor_copy(pairs_hi[:, :, i, b], both)
                v.drain()
                v.tensor_tensor(pairs_lo[:, :, i, b], both, pairs_hi[:, :, i, b], ALU.subtract)
                v.drain()
                v.nop().then_inc(used, 1)
            product(0, 0, first=True)
            product(0, 1)
            with v.Fori(1, NT // 2) as i:
                for b in range(2):
                    product(i, b)
            for t in range(NT):
                b = t % 2
                v.wait_ge(done, NT + t + 2)
                v.tensor_tensor(tmp[:, b], z[:, t], sk[:, :], ALU.mult)
                v.drain()
                v.tensor_tensor(tmp[:, b], tmp[:, b], pi[:, b], ALU.add)
                v.drain()
                v.tensor_tensor(out[:, t], tmp[:, b], gate[:, t], ALU.mult).then_inc(taken, 1)


def hyena(nc, conv, spec, skip, table, inv_table, ident, out):
    with ExitStack() as ctx:
        u = [ctx.enter_context(nc.sbuf_tensor(f"hy_u{k}", [P, NT, HY_W], F32)) for k in range(3)]
        for k in range(3):
            turn_back(nc, f"hyt{k}", conv[k * HY_W:(k + 1) * HY_W, :], u[k], ident)
        long_conv(nc, "lc0", u[0], u[1], spec[0], skip[0], table, inv_table, u[0])
        long_conv(nc, "lc1", u[0], u[2], spec[1], skip[1], table, inv_table, u[0])
        with Stage(nc, "hyo") as s:
            out_ok, block = s.sem("out_ok"), s.block()

            @block.sync
            def _(sp):
                sp.dma_start(rows(out), u[0][:, :, :]).then_inc(out_ok, 16)
                sp.wait_ge(out_ok, 16)


def turn_back(nc, name, src, dst, ident):
    with Stage(nc, name) as s:
        xt, ps = s.sb("xt", [P, 4, SEQ]), s.ps("ps", [P, 8, 512])
        x_in, turned, by_act, by_dve = (s.sem(n) for n in ("x_in", "turned", "by_act", "by_dve"))
        block = s.block()

        @block.sync
        def _(sp):
            sp.dma_start(xt[:, :, :], rows(src)).then_inc(x_in, 16)

        @block.tensor
        def _(pe):
            pe.wait_ge(x_in, 16)
            for t in range(NT):
                for q in range(4):
                    mm = pe.transpose(ps[:, t, q * P:q * P + P], xt[:, q, t * P:t * P + P], ident)
                mm.then_inc(turned, 1)

        @block.scalar
        def _(act):
            for t in range(0, NT, 2):
                act.wait_ge(turned, t + 1)
                act.activation(dst[:, t], ps[:, t], ACT.Copy).then_inc(by_act, 1)

        @block.vector
        def _(v):
            for t in range(1, NT, 2):
                v.wait_ge(turned, t + 1)
                v.tensor_copy(dst[:, t], ps[:, t]).then_inc(by_dve, 1)


E05 = float(np.exp(-0.5))
RK = 4


def rw_prepare(nc, conv, w0, w2, a0, a2, g2, k_k, k_a, r_k, tri, low, ones, ident, vecs, v_out, half, bonus, g_out):
    W, H, HD = RW_W, RW_H, RW_D
    R0 = HY_COLS
    with Stage(nc, "rp") as s:
        u = s.sb("u", [P, 2, 12, P])
        lr = s.sb("lr", [P, 2, 3, P])
        wt = s.sb("wt", [P, 2, 3, W])
        bias = s.sb("bias", [P, 4, W])
        rows3 = s.sb("rows3", [P, 3, W])
        r, k, v_, g = s.sb("r", [P, W]), s.sb("k", [P, W]), s.sb("v", [P, 2, W]), s.sb("g", [P, 2, W])
        kk, kn, ss, sr = s.sb("kk", [P, W]), s.sb("kn", [P, W]), s.sb("ss", [P, H]), s.sb("sr", [P, H])
        lw, aa = s.sb("lw", [P, 2, W]), s.sb("aa", [P, 2, W])
        hs, lc, lp = s.sb("hs", [P, 2, W]), s.sb("lc", [P, 2, W]), s.sb("lp", [P, 2, W])
        e1, e2, e3 = s.sb("e1", [P, 2, W]), s.sb("e2", [P, 2, W]), s.sb("e3", [P, 2, W])
        kd, t1, t2 = s.sb("kd", [P, W]), s.sb("t1", [P, W]), s.sb("t2", [P, W])
        vec = s.sb("vec", [P, 2, 2, RK, W])
        bs, bo = s.sb("bs", [P, 2, H]), s.sb("bo", [P, 2, W])
        hb = s.sb("hb", [1, 2, 2, W])
        p_t = [s.ps(f"p_t{n}", [P, W]) for n in range(3)]
        p_l = [s.ps(f"p_l{n}", [P, W]) for n in range(5)]
        c_in, loaded, nl = s.sem("c_in"), [s.sem(f"loaded{b}") for b in range(2)], s.sem("nl")
        stored = [s.sem(f"stored{b}") for b in range(2)]
        (turned, t_act, low_rank, pre, sig, lw_ok, cums, hs_ok, lexp_in, exps, vec_ok, norm_in, norm_root, done) = (
            s.sem(n) for n in ("turned", "t_act", "low_rank", "pre", "sig", "lw_ok", "cums", "hs_ok", "lexp_in", "exps",
                               "vec_ok", "norm_in", "norm_root", "done"))
        block = s.block()

        def tiles(eng, body):
            with eng.Fori(0, NT // 2) as i:
                for b in range(2):
                    body(i * 2 + b, b, i)

        def h3(ap):
            return ap.rearrange("p (h q) -> p h q", h=H)

        @block.sync
        def _(sp):
            for d in range(2):
                sp.dma_start(wt[64 * d:64 * d + 64, 0, 0], w2[d]).then_inc(c_in, 16)
                sp.dma_start(wt[64 * d:64 * d + 64, 0, 1], a2[d]).then_inc(c_in, 16)
                sp.dma_start(bias[:, d], w0[d].partition_broadcast(P)).then_inc(c_in, 16)
                sp.dma_start(bias[:, 2 + d], a0[d].partition_broadcast(P)).then_inc(c_in, 16)
            sp.dma_start(wt[:, 0, 2], g2).then_inc(c_in, 16)
            for n, src in enumerate((k_k, k_a, r_k)):
                sp.dma_start(rows3[:, n], src.partition_broadcast(P)).then_inc(c_in, 16)

            def load(j, b, i):
                sp.wait_ge(turned, j)
                sp.wait_ge(low_rank, j)
                sp.dma_start(u[:, b], conv[R0:R0 + 3 * W, :].rearrange("(c p) (i b t) -> i b p c t", p=P, b=2, t=P)[i, b]
                             ).then_inc(loaded[b], 16)
                sp.dma_start(lr[:, b], conv[R0 + 3 * W:R0 + RW_COLS, :].rearrange("(c p) (i b t) -> i b p c t", p=P, b=2, t=P)[i, b]
                             ).then_inc(loaded[b], 16)
            tiles(sp, load)

        @block.tensor
        def _(pe):
            pe.nop().then_inc(turned, 1)
            pe.nop().then_inc(low_rank, 1)
            pe.wait_ge(c_in, 12 * 16)

            def step(j, b, i):
                pe.wait_ge(loaded[b], i * 32 + 32)
                pe.wait_ge(t_act, j * 3)
                for n in range(3):
                    for q in range(4):
                        mm = pe.transpose(p_t[n][:, q * P:q * P + P], u[:, b, 4 * n + q], ident)
                mm.then_inc(turned, 1)
                pe.wait_ge(nl, j + 1)
                pe.wait_ge(lexp_in, j)
                for d in range(2):
                    pe.matmul(p_l[d][:, :], lr[64 * d:64 * d + 64, b, 0], wt[64 * d:64 * d + 64, 0, 0], start=True, stop=True)
                    pe.matmul(p_l[2 + d][:, :], lr[64 * d:64 * d + 64, b, 1], wt[64 * d:64 * d + 64, 0, 1], start=True, stop=True)
                pe.matmul(p_l[4][:, :], lr[:, b, 2], wt[:, 0, 2], start=True, stop=True).then_inc(low_rank, 1)
                pe.wait_ge(lw_ok, j + 1)
                for d in range(2):
                    pe.matmul(p_l[d][:, :], low if d else tri, lw[:, d], start=True, stop=True)
                    mm = pe.matmul(p_l[2 + d][:, :], ones, lw[:, d], start=True, stop=True)
                mm.then_inc(cums, 1)
            tiles(pe, step)

        @block.scalar
        def _(act):
            def step(j, b, i):
                act.wait_ge(loaded[b], i * 32 + 32)
                act.activation(lr[:, b, 0], lr[:, b, 0], ACT.Tanh)
                act.activation(lr[:, b, 2], lr[:, b, 2], ACT.Sigmoid)
                act.drain()
                act.nop().then_inc(nl, 1)
                act.wait_ge(turned, j + 2)
                act.wait_ge(done, j)
                act.wait_ge(stored[b], i * 96)
                for n, t in enumerate((r[:, :], k[:, :], v_[:, b])):
                    act.activation(t, p_t[n][:, :], ACT.Copy).then_inc(t_act, 1)
                act.wait_ge(pre, j + 1)
                act.activation(g[:, b], p_l[4][:, :], ACT.Copy)
                act.activation(aa[:, :, :], aa[:, :, :], ACT.Sigmoid)
                act.activation(lw[:, :, :], lw[:, :, :], ACT.Sigmoid).then_inc(sig, 1)
                act.wait_ge(norm_in, j + 1)
                act.activation(sr[:, :], ss[:, :], ACT.Sqrt).then_inc(norm_root, 1)
                act.wait_ge(cums, j + 1)
                for d in range(2):
                    last = act.activation(hs[:, d], p_l[2 + d][:, :], ACT.Copy, scale=0.5)
                last.then_inc(hs_ok, 1)
                act.wait_ge(lexp_in, j + 1)
                act.activation(e1[:, :, :], lc[:, :, :], ACT.Exp)
                act.activation(e2[:, :, :], lp[:, :, :], ACT.Exp)
                act.activation(e3[:, :, :], lc[:, :, :], ACT.Exp, scale=-1.0).then_inc(exps, 1)
            tiles(act, step)

        @block.vector
        def _(v):
            v.wait_ge(c_in, 12 * 16)

            def step(j, b, i):
                v.wait_ge(low_rank, j + 2)
                for d in range(2):
                    v.tensor_tensor(lw[:, d], p_l[d][:, :], bias[:, d], ALU.add)
                    v.tensor_tensor(aa[:, d], p_l[2 + d][:, :], bias[:, 2 + d], ALU.add)
                v.drain()
                v.nop().then_inc(pre, 1)
                v.wait_ge(t_act, j * 3 + 3)
                v.tensor_tensor(kk[:, :], k[:, :], rows3[:, 0], ALU.mult)
                v.drain()
                v.tensor_tensor(kn[:, :], kk[:, :], kk[:, :], ALU.mult)
                v.drain()
                v.tensor_reduce(ss[:, :], h3(kn[:, :]), AXX, ALU.add)
                v.drain()
                v.nop().then_inc(norm_in, 1)
                v.wait_ge(sig, j + 1)
                v.tensor_scalar(lw[:, :, :], lw[:, :, :], -E05, None, ALU.mult).then_inc(lw_ok, 1)
                v.wait_ge(norm_root, j + 1)
                v.tensor_scalar(ss[:, :], sr[:, :], 1e-12, None, ALU.max)
                v.drain()
                v.reciprocal(ss[:, :], ss[:, :])
                v.drain()
                v.tensor_tensor(h3(kk[:, :]), h3(kk[:, :]), bc(ss[:, :].unsqueeze(2), [P, H, HD]), ALU.mult)
                v.wait_ge(hs_ok, j + 1)
                for d in range(2):
                    v.tensor_tensor(lc[:, d], p_l[d][:, :], hs[:, d], ALU.subtract)
                v.drain()
                v.tensor_tensor(lp[:, :, :], lc[:, :, :], lw[:, :, :], ALU.subtract).then_inc(lexp_in, 1)
                v.wait_ge(stored[b], i * 96)
                v.tensor_copy(hb[:, b], hs[0:1, :, :])
                v.drain()
                v.wait_ge(exps, j + 1)
                for d in range(2):
                    if d:
                        v.drain()
                    v.scalar_tensor_tensor(t1[:, :], aa[:, d], -1.0, rows3[:, 1], ALU.add, ALU.mult)
                    v.drain()
                    v.scalar_tensor_tensor(kd[:, :], t1[:, :], 1.0, k[:, :], ALU.add, ALU.mult)
                    v.tensor_tensor(t2[:, :], kk[:, :], aa[:, d], ALU.mult)
                    v.drain()
                    v.tensor_tensor(vec[:, b, d, 0], kk[:, :], e2[:, d], ALU.mult)
                    v.tensor_tensor(vec[:, b, d, 1], r[:, :], e1[:, d], ALU.mult)
                    v.tensor_tensor(vec[:, b, d, 2], t2[:, :], e3[:, d], ALU.mult)
                    v.tensor_tensor(vec[:, b, d, 3], kd[:, :], e3[:, d], ALU.mult)
                    v.tensor_tensor(t1[:, :], kd[:, :], r[:, :], ALU.mult)
                    v.drain()
                    v.nop().then_inc(vec_ok, 1)
                    v.tensor_tensor(t1[:, :], t1[:, :], rows3[:, 2], ALU.mult)
                    v.drain()
                    v.tensor_reduce(bs[:, d], h3(t1[:, :]), AXX, ALU.add)
                v.drain()
                v.tensor_tensor(bs[:, 0], bs[:, 0], bs[:, 1], ALU.add)
                v.drain()
                v.tensor_tensor(h3(bo[:, b]), h3(v_[:, b]), bc(bs[:, 0].unsqueeze(2), [P, H, HD]), ALU.mult)
                v.drain()
                v.nop().then_inc(done, 1)
            tiles(v, step)

        @block.gpsimd
        def _(pool):
            def store(j, b, i):
                for d in range(2):
                    pool.wait_ge(vec_ok, j * 2 + (d + 1))
                    pool.dma_start(vecs[d].rearrange("(i b p) k n -> i b p k n", b=2, p=P)[i, b], vec[:, b, d]).then_inc(stored[b], 16)
                pool.wait_ge(done, j + 1)
                pool.dma_start(half.rearrange("d (i b a) n -> i b a d n", b=2, a=1)[i, b], hb[:, b]).then_inc(stored[b], 16)
                for dst, src in ((v_out, v_), (g_out, g), (bonus, bo)):
                    pool.dma_start(dst.rearrange("(i b p) n -> i b p n", b=2, p=P)[i, b], src[:, b]).then_inc(stored[b], 16)
            tiles(pool, store)
            for b in range(2):
                pool.wait_ge(stored[b], NT // 2 * 96)


def rw_scan(nc, vecs, v_in, half, masks, n_masks, ident, y_out):
    W, H, HD = RW_W, RW_H, RW_D
    NG, LV = 4, 6
    with Stage(nc, "rs") as s:
        vec, vt = s.sb("vec", [P, 2, 2, RK, W]), s.sb("vt", [P, 2, 2, W])
        mk, mn = s.sb("mk", [P, 2, 4, P]), s.sb("mn", [P, 2, P])
        eh = s.sb("eh", [P, 2, 2, 4])
        chm = s.sb("chm", [P, 2, 4, RK, P])
        m4 = s.sb("m4", [P, 2 * H, 4, P])
        power = [s.sb(f"power{n}", [P, NG, 2, 4, P]) for n in range(2)]
        xt = s.sb("xt", [P, NG, 4, P])
        zs, us = s.sb("zs", [P, 2, W]), s.sb("us", [P, 2, W])
        st, sd = s.sb("st", [P, 2, 4, HD]), s.sb("sd", [P, 2, 4, HD])
        ys = s.sb("ys", [P, 2, 2, W])
        p_t = [s.ps(f"p_t{n}", [P, 4, P]) for n in range(2)]
        p_n = [s.ps(f"p_n{n}", [P, 4, P]) for n in range(2)]
        p_q = [s.ps(f"p_q{n}", [P, 4, P]) for n in range(2)]
        p_x = [s.ps(f"p_x{n}", [P, 4, P]) for n in range(2)]
        m_in, loaded = s.sem("m_in"), [s.sem(f"loaded{b}") for b in range(2)]
        stored = [s.sem(f"stored{b}") for b in range(2)]
        (turned, t_act, t_dve, scored, masked, n_done, n_masked, x_init, squared, q_act, q_dve, xmul, x_ok, eh_ok,
         s_scaled, z_done, z_ok, u_done, u_ok, y_done, y_act, y_dve, d_done, s_ok) = (s.sem(n) for n in (
             "turned", "t_act", "t_dve", "scored", "masked", "n_done", "n_masked", "x_init", "squared", "q_act", "q_dve",
             "xmul", "x_ok", "eh_ok", "s_scaled", "z_done", "z_ok", "u_done", "u_ok", "y_done", "y_act", "y_dve",
             "d_done", "s_ok"))
        block = s.block()

        def steps(eng, body):
            with eng.Fori(0, NCH // 2) as i:
                for b in range(2):
                    body(i * 2 + b, b, i)

        def flat(ap):
            return ap.rearrange("p a n -> p (a n)")

        def by_head(ap):
            return ap.rearrange("p d (q o n) -> p (d q) n o", o=2, n=HD)

        units = [(odd, d, q, d * H + odd * 4 + q, 64 * odd, slice((4 * d + q) * HD, (4 * d + q) * HD + HD),
                  slice((2 * q + odd) * HD, (2 * q + odd) * HD + HD))
                 for odd in range(2) for d in range(2) for q in range(4)]

        @block.sync
        def _(sp):
            sp.dma_start(mk[:, :, :, :], masks.rearrange("d a p n -> p d a n")).then_inc(m_in, 16)
            sp.dma_start(mn[:, :, :], n_masks.rearrange("d p n -> p d n")).then_inc(m_in, 16)

            def load(j, b, i):
                sp.wait_ge(s_ok, j)
                for d in range(2):
                    c = j if d == 0 else (NCH - 1) - j
                    sp.dma_start(vec[:, b, d], vecs[d].rearrange("(j p) k n -> j p k n", p=P)[c]).then_inc(loaded[b], 16)
                    sp.dma_start(vt[:, b, d], v_in.rearrange("(j p) n -> j p n", p=P)[c]).then_inc(loaded[b], 16)
                    sp.dma_start(eh[:, b, d], half[d].rearrange("c (q p) -> c p q", p=P)[c],
                                 allow_slow_non_contiguous=True).then_inc(loaded[b], 16)
            steps(sp, load)

        @block.tensor
        def _(pe):
            def step(j, b, i):
                pe.wait_ge(loaded[b], i * 96 + 96)
                pe.wait_ge(masked, j * 16 + 2)
                for n in range(8):
                    pe.wait_ge(t_dve if n % 2 else t_act, j * 4 + n // 2)
                    for k in range(RK):
                        mm = pe.transpose(p_t[n % 2][:, k], vec[:, b, n // 4, k, (n % 4) * P:(n % 4) * P + P], ident)
                    mm.then_inc(turned, 1)
                pe.wait_ge(t_act, j * 4 + 4)
                pe.wait_ge(t_dve, j * 4 + 4)
                for un in range(2 * H):
                    d, q, o = un // H, un % 4, 64 * ((un // 4) % 2)
                    pe.wait_ge(masked, j * 16 + (un + 1))
                    kr = flat(chm[o:o + 64, d, q, 0:2])
                    pe.matmul(flat(p_t[un % 2][:, 0:2]), chm[o:o + 64, d, q, 2], kr, start=True, stop=True)
                    pe.matmul(flat(p_t[un % 2][:, 2:4]), chm[o:o + 64, d, q, 3], kr, start=True, stop=True).then_inc(scored, 1)
                pe.wait_ge(q_act, j * (LV * NG) + 2)
                for g in range(NG):
                    if g >= 2:
                        pe.wait_ge(n_masked, j * NG + (g - 1))
                    for k in range(4):
                        d, o = g // 2, 64 * (g % 2)
                        mm = pe.matmul(p_n[g % 2][:, k], chm[o:o + 64, d, k, 0], chm[o:o + 64, d, k, 2], start=True, stop=True)
                    mm.then_inc(n_done, 1)
                pe.wait_ge(n_masked, j * NG + NG)
                pe.wait_ge(masked, j * 16 + 18)
                pe.wait_ge(y_act, j)
                pe.wait_ge(y_dve, j)
                pe.wait_ge(s_ok, j + 1)
                for lv in range(LV):
                    src, dst = power[lv % 2], power[1 - lv % 2]
                    for g in range(NG):
                        n = j * (LV * NG) + (lv * NG + g)
                        pe.wait_ge(q_act, n + 1)
                        pe.wait_ge(q_dve, n + 1)
                        for k in range(4):
                            nt = src[:, g, 1, k] if lv else m4[:, 4 * g + k, 0]
                            mm = pe.matmul(p_n[g % 2][:, k], nt, src[:, g, 0, k], start=True, stop=True)
                        for k in range(4) if lv < LV - 1 else ():
                            nt = src[:, g, 1, k] if lv else m4[:, 4 * g + k, 0]
                            mm = pe.matmul(p_q[g % 2][:, k], src[:, g, 0, k], nt, start=True, stop=True)
                        mm.then_inc(squared, 1)
                    for g in range(NG):
                        n = j * (LV * NG) + (lv * NG + g)
                        pe.wait_ge(q_act, n + 3)
                        pe.wait_ge(x_ok, n + 1)
                        if lv == 0:
                            pe.wait_ge(x_init, j * NG + (g + 1))
                        for k in range(4):
                            mm = pe.matmul(p_x[g % 2][:, k], dst[:, g, 0, k], xt[:, g, k], start=True, stop=True)
                        mm.then_inc(xmul, 1)
                pe.wait_ge(s_scaled, j + 1)
                for odd, d, q, un, o, c, hc in units:
                    pe.matmul(flat(p_t[odd][:, :])[:, c], chm[o:o + 64, d, q, 0], sd[o:o + 64, d, q], start=True, stop=False)
                    mm = pe.matmul(flat(p_t[odd][:, :])[:, c], m4[:, un, 2], vt[:, b, d, hc], start=False, stop=True)
                mm.then_inc(z_done, 1)
                pe.wait_ge(z_ok, j + 1)
                pe.wait_ge(x_ok, (j + 1) * (LV * NG) + 2)
                pe.wait_ge(q_act, (j + 1) * (LV * NG) + 2)
                pe.wait_ge(q_dve, (j + 1) * (LV * NG) + 2)
                for odd, d, q, un, o, c, hc in units:
                    mm = pe.matmul(flat(p_n[odd][:, :])[:, c], xt[:, un // 4, un % 4], zs[:, odd, c], start=True, stop=True)
                mm.then_inc(u_done, 1)
                pe.wait_ge(u_ok, j + 1)
                for odd, d, q, un, o, c, hc in units:
                    pe.matmul(flat(p_q[odd][:, :])[:, c], chm[o:o + 64, d, q, 1], sd[o:o + 64, d, q], start=True, stop=False)
                    pe.matmul(flat(p_q[odd][:, :])[:, c], m4[:, un, 1], us[:, odd, c], start=False, stop=False)
                    mm = pe.matmul(flat(p_q[odd][:, :])[:, c], m4[:, un, 3], vt[:, b, d, hc], start=False, stop=True)
                mm.then_inc(y_done, 1)
                for odd, d, q, un, o, c, hc in units:
                    out = flat(p_x[0][o:o + 64])[:, c]
                    pe.matmul(out, vec[:, b, d, 2, hc], us[:, odd, c], start=True, stop=False)
                    mm = pe.matmul(out, vec[:, b, d, 3, hc], vt[:, b, d, hc], start=False, stop=True)
                mm.then_inc(d_done, 1)
            steps(pe, step)

        @block.scalar
        def _(act):
            act.nop().then_inc(q_act, 2)

            def step(j, b, i):
                act.wait_ge(loaded[b], i * 96 + 96)
                act.activation(eh[:, b], eh[:, b], ACT.Exp).then_inc(eh_ok, 1)
                for n in range(0, 8, 2):
                    act.wait_ge(turned, j * 8 + (n + 1))
                    act.activation(chm[:, n // 4, n % 4], p_t[0][:, :, :], ACT.Copy).then_inc(t_act, 1)
                for lv in range(LV):
                    for g in range(NG):
                        act.wait_ge(squared, j * (LV * NG) + (lv * NG + g + 1))
                        act.activation(power[1 - lv % 2][:, g, 0], p_n[g % 2][:, :, :], ACT.Copy).then_inc(q_act, 1)
                act.wait_ge(z_done, j + 1)
                for d in range(2):
                    last = act.activation(zs[:, d], flat(p_t[d][:, :]), ACT.Copy)
                last.then_inc(z_ok, 1)
                act.wait_ge(u_done, j + 1)
                for d in range(2):
                    last = act.activation(us[:, d], flat(p_n[d][:, :]), ACT.Copy, scale=-1.0)
                last.then_inc(u_ok, 1)
                act.wait_ge(y_done, j + 1)
                act.wait_ge(stored[b], i * 32)
                act.activation(by_head(ys[:, b])[:, :, :, 0], p_q[0][:, :, :].rearrange("p a (c n) -> p (a c) n", n=HD),
                               ACT.Copy).then_inc(y_act, 1)
            steps(act, step)

        @block.vector
        def _(v):
            v.memset(st[:, :, :, :], 0.0)
            v.nop().then_inc(masked, 2)
            v.nop().then_inc(q_dve, 2)
            v.nop().then_inc(x_ok, 2)
            v.drain()
            v.nop().then_inc(s_ok, 1)
            v.wait_ge(m_in, 32)

            def step(j, b, i):
                for n in range(1, 8, 2):
                    v.wait_ge(turned, j * 8 + (n + 1))
                    v.tensor_copy(chm[:, n // 4, n % 4], p_t[1][:, :, :]).then_inc(t_dve, 1)
                v.wait_ge(eh_ok, j + 1)
                v.tensor_tensor(sd[:, :, :, :], st[:, :, :, :], bc(eh[:, b].unsqueeze(3), [P, 2, 4, HD]),
                                ALU.mult).then_inc(s_scaled, 1)
                for un in range(2 * H):
                    v.wait_ge(scored, j * 16 + (un + 1))
                    v.tensor_tensor(m4[:, un], p_t[un % 2][:, :, :], mk[:, un // H], ALU.mult).then_inc(masked, 1)
                for g in range(NG):
                    v.wait_ge(n_done, j * NG + (g + 1))
                    v.tensor_tensor(power[0][:, g, 0], p_n[g % 2][:, :, :], bc(mn[:, g // 2].unsqueeze(1), [P, 4, P]),
                                    ALU.mult).then_inc(n_masked, 1)
                v.drain()
                for g in range(NG):
                    v.tensor_tensor(xt[:, g], m4[:, 4 * g:4 * g + 4, 0], bc(ident.unsqueeze(1), [P, 4, P]),
                                    ALU.add).then_inc(x_init, 1)
                for lv in range(LV):
                    for g in range(NG):
                        v.wait_ge(squared, j * (LV * NG) + (lv * NG + g + 1))
                        if lv < LV - 1:
                            v.tensor_copy(power[1 - lv % 2][:, g, 1], p_q[g % 2][:, :, :]).then_inc(q_dve, 1)
                        else:
                            v.nop().then_inc(q_dve, 1)
                    v.drain()
                    for g in range(NG):
                        v.wait_ge(xmul, j * (LV * NG) + (lv * NG + g + 1))
                        v.tensor_tensor(xt[:, g], xt[:, g], p_x[g % 2][:, :, :], ALU.add).then_inc(x_ok, 1)
                v.wait_ge(y_done, j + 1)
                v.wait_ge(stored[b], i * 32)
                v.tensor_copy(by_head(ys[:, b])[:, :, :, 1], p_q[1][:, :, :].rearrange("p a (c n) -> p (a c) n", n=HD)
                              ).then_inc(y_dve, 1)
                v.wait_ge(d_done, j + 1)
                v.tensor_tensor(sd[:, :, :, :].rearrange("p d q n -> p (d q n)"),
                                sd[:, :, :, :].rearrange("p d q n -> p (d q n)"), flat(p_x[0][:, :]), ALU.add)
                v.drain()
                v.tensor_tensor(st[:, :, :, :], sd[:, :, :, :], bc(eh[:, b].unsqueeze(3), [P, 2, 4, HD]), ALU.mult)
                v.drain()
                v.nop().then_inc(s_ok, 1)
            steps(v, step)

        @block.gpsimd
        def _(pool):
            def store(j, b, i):
                pool.wait_ge(y_dve, j + 1)
                pool.wait_ge(y_act, j + 1)
                for d in range(2):
                    pool.dma_start(y_out[d].rearrange("(i b p) n -> i b p n", b=2, p=P)[i, b], ys[:, b, d]).then_inc(stored[b], 16)
            steps(pool, store)
            for b in range(2):
                pool.wait_ge(stored[b], NCH // 2 * 32)


def rw_finish(nc, y_in, bonus, g_in, gn_w, gn_b, out):
    W, H, HD = RW_W, RW_H, RW_D
    with Stage(nc, "rf") as s:
        y, y2, bo, g = (s.sb(n, [P, NT, W]) for n in ("y", "y2", "bo", "g"))
        gw, gb, sq = s.sb("gw", [P, W]), s.sb("gb", [P, W]), s.sb("sq", [P, NT, W])
        mean, var, rs = s.sb("mean", [P, NT, H]), s.sb("var", [P, NT, H]), s.sb("rs", [P, NT, H])
        NG = 4
        GT = NT // NG
        got = [s.sem(f"got{n}") for n in range(NG)]
        w_in, biased, centred, squares, var_ok, root, done, out_ok = (s.sem(n) for n in (
            "w_in", "biased", "centred", "squares", "var_ok", "root", "done", "out_ok"))
        block = s.block()

        def heads(ap, n):
            return ap[:, n * GT:(n + 1) * GT].rearrange("p t (h q) -> p (t h) q", h=H)

        def all_of(ap, n):
            return ap[:, n * GT:(n + 1) * GT]

        def stats(ap, n):
            return ap[:, n * GT:(n + 1) * GT].rearrange("p t h -> p (t h)")

        @block.sync
        def _(sp):
            for t, src in ((gw, gn_w), (gb, gn_b)):
                sp.dma_start(t[:, :], src.partition_broadcast(P)).then_inc(w_in, 16)
            for n in range(NG):
                for t, src in ((y, y_in[0]), (bo, bonus), (g, g_in)):
                    sp.dma_start(all_of(t, n), all_of(rows(src), n)).then_inc(got[n], 16)
                for t in range(n * GT, (n + 1) * GT):
                    sp.dma_start(y2[:, t], y_in[1][(NT - 1 - t) * P:(NT - t) * P, :]).then_inc(got[n], 16)
            for n in range(NG):
                sp.wait_ge(done, n + 1)
                sp.dma_start(all_of(rows(out), n), all_of(y, n)).then_inc(out_ok, 16)
            sp.wait_ge(out_ok, 16 * NG)

        @block.scalar
        def _(act):
            for n in range(NG):
                act.wait_ge(centred, n + 1)
                act.activation(all_of(sq, n), all_of(y, n), ACT.Square).then_inc(squares, 1)
                act.wait_ge(var_ok, n + 1)
                act.activation(stats(rs, n), stats(var, n), ACT.Sqrt).then_inc(root, 1)

        @block.gpsimd
        def _(pool):
            pool.wait_ge(w_in, 32)
            for n in range(NG):
                pool.wait_ge(got[n], 16 * (3 + GT))
                pool.tensor_tensor(all_of(bo, n), all_of(bo, n), bc(gb[:, :].unsqueeze(1), [P, GT, W]), ALU.add).then_inc(biased, 1)

        @block.vector
        def _(v):
            def centre(n):
                v.wait_ge(got[n], 16 * (3 + GT))
                v.tensor_tensor(all_of(y, n), all_of(y, n), all_of(y2, n), ALU.add)
                v.drain()
                v.tensor_reduce(stats(mean, n), heads(y, n), AXX, ALU.add)
                v.drain()
                v.tensor_scalar(stats(mean, n), stats(mean, n), 1.0 / HD, None, ALU.mult)
                v.drain()
                v.tensor_tensor(heads(y, n), heads(y, n), bc(stats(mean, n).unsqueeze(2), [P, GT * H, HD]), ALU.subtract)
                v.drain()
                v.nop().then_inc(centred, 1)

            def finish(n):
                v.wait_ge(squares, n + 1)
                v.tensor_reduce(stats(var, n), heads(sq, n), AXX, ALU.add)
                v.drain()
                v.tensor_scalar(stats(var, n), stats(var, n), 1.0 / HD, RW_GN_EPS, ALU.mult, ALU.add).then_inc(var_ok, 1)
                v.wait_ge(root, n + 1)
                v.reciprocal(stats(rs, n), stats(rs, n))
                v.drain()
                v.tensor_tensor(heads(y, n), heads(y, n), bc(stats(rs, n).unsqueeze(2), [P, GT * H, HD]), ALU.mult)
                v.drain()
                v.tensor_tensor(all_of(y, n), all_of(y, n), bc(gw[:, :].unsqueeze(1), [P, GT, W]), ALU.mult)
                v.drain()
                v.wait_ge(biased, n + 1)
                v.tensor_tensor(all_of(y, n), all_of(y, n), all_of(bo, n), ALU.add)
                v.drain()
                v.tensor_tensor(all_of(y, n), all_of(y, n), all_of(g, n), ALU.mult).then_inc(done, 1)
            v.wait_ge(w_in, 32)
            for n in range(NG):
                centre(n)
                if n:
                    finish(n - 1)
            finish(NG - 1)


def gate_mix(nc, name, gates_in, yh, yr, ident, dst_t):
    with Stage(nc, name) as s:
        gt, a, b_ = s.sb("gt", [P, NT, 2, D]), s.sb("a", [P, NT, D]), s.sb("b", [P, NT, D])
        ps = s.ps("ps", [P, 2, 8, P])
        loaded = [s.sem(f"loaded{t}") for t in range(NT)]
        sig, mixed, turned, by_act, by_dve = (s.sem(n) for n in ("sig", "mixed", "turned", "by_act", "by_dve"))
        block = s.block()

        @block.sync
        def _(sp):
            for t in range(NT):
                k = t
                sl = slice(t * P, (t + 1) * P)
                sp.dma_start(gt[:, k], gates_in[sl, :].rearrange("p (a n) -> p a n", a=2)).then_inc(loaded[k], 16)
                sp.dma_start(a[:, k], yh[sl, :]).then_inc(loaded[k], 16)
                sp.dma_start(b_[:, k], yr[sl, :]).then_inc(loaded[k], 16)

        @block.scalar
        def _(act):
            for t in range(NT):
                k = t
                act.wait_ge(loaded[k], 48)
                act.activation(gt[:, k], gt[:, k], ACT.Sigmoid).then_inc(sig, 1)
                act.wait_ge(turned, t + 1)
                act.activation(dst_t[:, 0:4, t * P:t * P + P], ps[:, t % 2, 0:4], ACT.Copy).then_inc(by_act, 1)

        @block.vector
        def _(v):
            for t in range(NT):
                k = t
                v.wait_ge(sig, t + 1)
                v.tensor_tensor(a[:, k], a[:, k], gt[:, k, 0], ALU.mult)
                v.tensor_tensor(b_[:, k], b_[:, k], gt[:, k, 1], ALU.mult)
                v.drain()
                v.tensor_tensor(a[:, k], a[:, k], b_[:, k], ALU.add).then_inc(mixed, 1)
                v.wait_ge(turned, t + 1)
                v.tensor_copy(dst_t[:, 4:8, t * P:t * P + P], ps[:, t % 2, 4:8]).then_inc(by_dve, 1)

        @block.tensor
        def _(pe):
            for t in range(NT):
                pe.wait_ge(mixed, t + 1)
                if t >= 2:
                    pe.wait_ge(by_act, t - 1)
                    pe.wait_ge(by_dve, t - 1)
                for c in range(8):
                    mm = pe.transpose(ps[:, t % 2, c], a[:, t, c * P:c * P + P], ident)
                mm.then_inc(turned, 1)


def ffn_up(nc, x_half, w_gate, w_up, hT):
    KT, NU = D // P, FFN_H // P
    with Stage(nc, "fu") as s:
        w, one = s.sb("w", [P, 2, KT, P]), s.sb("one", [P, 1])
        w_hi, w_lo = (s.sb(n, [P, 2, 2, KT, P], HALF) for n in ("w_hi", "w_lo"))
        x_hi, x_lo = x_half
        sg = s.sb("sg", [P, 2, SEQ])
        ps = s.ps("ps", [P, 2, 2, SEQ])
        w_in, gated, upped, sig, used, split = (s.sem(n) for n in ("w_in", "gated", "upped", "sig", "used", "split"))
        block = s.block()

        def units(eng, body):
            with eng.Fori(0, NU // 2) as i:
                for b in range(2):
                    body(i * 2 + b, b, i)

        @block.sync
        def _(sp):
            def load(j, b, i):
                sp.wait_ge(split, j + 1)
                for k, src in enumerate((w_gate, w_up)):
                    sp.dma_start(w[:, k], src.rearrange("(k p) (i b n) -> i b p k n", p=P, b=2, n=P)[i, b]).then_inc(w_in, 16)
            units(sp, load)

        @block.tensor
        def _(pe):
            pe.nop().then_inc(upped, 1)

            def step(j, b, i):
                pe.wait_ge(split, j + 2)
                pe.wait_ge(used, j)
                for kind in range(2):
                    for h in range(2):
                        for k in range(KT):
                            mm = products3(pe, ps[:, b, kind, h * 512:h * 512 + 512],
                                           [a[:, b, kind, k] for a in (w_hi, w_lo)],
                                           [a[:, k, h * 512:h * 512 + 512] for a in (x_hi, x_lo)], k, KT)
                    mm.then_inc(upped if kind else gated, 1)
            units(pe, step)

        @block.gpsimd
        def _(pool):
            pool.nop().then_inc(split, 1)
            pool.memset(one[:, :], 1.0)
            pool.drain()

            def halve(j, b, i):
                pool.wait_ge(w_in, j * 32 + 32)
                pool.wait_ge(upped, j)
                halves_on_pool(pool, w[:, :, :, :], w_hi[:, b], w_lo[:, b], one, [P, 2, KT, P]).then_inc(split, 1)
            units(pool, halve)

        @block.scalar
        def _(act):
            def step(j, b, i):
                act.wait_ge(gated, j + 1)
                act.wait_ge(used, j)
                act.activation(sg[:, b], ps[:, b, 0], ACT.Silu).then_inc(sig, 1)
            units(act, step)

        @block.vector
        def _(v):
            v.nop().then_inc(used, 1)
            out = hT[:, :, :].rearrange("p (i b) t -> p i b t", b=2)

            def step(j, b, i):
                v.wait_ge(sig, j + 1)
                v.wait_ge(upped, j + 2)
                v.tensor_tensor(out[:, i, b], sg[:, b], ps[:, b, 1], ALU.mult).then_inc(used, 1)
            units(v, step)


def gemm_deep(nc, name, aT, w_src, out, n_out=4):
    KT = aT.shape[1]
    with Stage(nc, name) as s:
        w, o, one = s.sb("w", [P, 2, 2, 512]), s.sb("o", [P, n_out, 2, 512]), s.sb("one", [P, 1])
        w_hi, w_lo = (s.sb(n, [P, 2, 2, 512], HALF) for n in ("w_hi", "w_lo"))
        a_hi, a_lo = (s.sb(n, [P, 2, SEQ], HALF) for n in ("a_hi", "a_lo"))
        ps = s.ps("ps", [P, NT, 512])
        w_in = [s.sem(f"w_in{b}") for b in range(2)]
        stored = [s.sem(f"stored{b}") for b in range(n_out)]
        used, done, by_act, by_dve, split, high, low = (s.sem(n) for n in (
            "used", "done", "by_act", "by_dve", "split", "high", "low"))
        block = s.block()
        NL = KT // 2

        def free(eng, m):
            if m >= 2 and (m - 2) % KT == KT - 1:
                eng.wait_ge(done, NT)
            elif m >= 2:
                eng.wait_ge(used, m - 1 - (m - 2) // KT)

        @block.sync
        def _(sp):
            for n in range(2 * NL):
                c, l = n // NL, n % NL
                free(sp, 2 * n - 1)
                sp.dma_start(w[:, n % 2], rows(w_src)[:, 2 * l:2 * l + 2, c * 512:c * 512 + 512]).then_inc(w_in[n % 2], 16)

        @block.gpsimd
        def _(pool):
            pool.memset(one[:, :], 1.0)
            pool.drain()
            for n in range(2 * NL):
                pool.wait_ge(w_in[n % 2], 16 * (n // 2 + 1))
                free(pool, 2 * n - 1)
                halves_on_pool(pool, w[:, n % 2], w_hi[:, n % 2], w_lo[:, n % 2], one, [P, 2, 512]).then_inc(split, 1)

        @block.tensor
        def _(pe):
            for n in range(2 * NL):
                c, l = n // NL, n % NL
                pe.wait_ge(split, n + 1)
                for k in range(2):
                    kk = 2 * l + k
                    pe.wait_ge(low, 2 * n + k + 1)
                    for t in range(NT):
                        if c and kk == 0:
                            pe.wait_ge(by_dve if t % 2 else by_act, t // 2 + 1)
                        mm = products3(pe, ps[:, t], [a[:, k, t * P:t * P + P] for a in (a_hi, a_lo)],
                                       [a[:, n % 2, k] for a in (w_hi, w_lo)], kk, KT)
                        if kk == KT - 1:
                            mm.then_inc(done, 1)
                        elif t == NT - 1:
                            mm.then_inc(used, 1)

        def take(eng, odd, sem, c):
            for t in range(0, NT, 2):
                n = (c * NT + t) // 2
                eng.wait_ge(done, c * NT + t + odd + 1)
                b = n % n_out
                if n >= n_out:
                    eng.wait_ge(stored[b], 16 * (n // n_out))
                if odd:
                    eng.tensor_copy(o[:, b, 1], ps[:, t + 1]).then_inc(sem, 1)
                    continue
                eng.activation(o[:, b, 0], ps[:, t], ACT.Copy).then_inc(sem, 1)
                eng.wait_ge(by_act, n + 1)
                eng.wait_ge(by_dve, n + 1)
                eng.dma_start(rows(out)[:, t:t + 2, c * 512:c * 512 + 512], o[:, b]).then_inc(stored[b], 16)

        def work(eng, odd, sem):
            for m in range(2 * KT):
                if m == KT:
                    take(eng, odd, sem, 0)
                free(eng, m)
                src, hi, lo = aT[:, m % KT], a_hi[:, m % 2], a_lo[:, m % 2]
                if odd:
                    eng.wait_ge(high, m + 1)
                    eng.tensor_tensor(lo, src, hi, ALU.subtract).then_inc(low, 1)
                else:
                    eng.activation(hi, src, ACT.Copy).then_inc(high, 1)
            take(eng, odd, sem, 1)

        @block.scalar
        def _(act):
            work(act, 0, by_act)
            for b in range(n_out):
                act.wait_ge(stored[b], 16 * NT // n_out)

        @block.vector
        def _(v):
            work(v, 1, by_dve)


def constants():
    f32 = np.float32
    tri = np.triu(np.ones((P, P), f32))
    c = {
        "c_ident": np.eye(P, dtype=f32), "c_tri": tri, "c_strict": np.triu(np.ones((P, P), f32), 1),
        "c_ones": np.ones((P, P), f32), "c_neg": np.tril(np.full((P, P), -BIG, f32), -1),
        "c_low": np.ascontiguousarray(tri.T), "c_slow": np.tril(np.ones((P, P), f32), -1),
        "c_iota": np.arange(64, dtype=f32),
    }
    up, upi, lo_, loi = c["c_strict"], c["c_tri"], c["c_slow"], c["c_low"]
    c["c_masks"] = np.stack([np.stack([-up, upi, up, upi]), np.stack([-lo_, loi, lo_, loi])])
    c["c_nmasks"] = np.stack([-lo_, -up])
    t = np.arange(SEQ)
    cos = np.cos(2 * np.pi * ((t[:, None] * t[None, :]) % NF) / NF)
    sin = np.sin(2 * np.pi * ((t[:, None] * t[None, :]) % NF) / NF)
    sin[:, 0] = 1.0 - 2.0 * (t % 2)
    tab = np.stack([cos, sin])
    c["c_dft"] = np.ascontiguousarray(tab.reshape(2, NT, P, NT, P).transpose(3, 0, 2, 1, 4)).astype(f32)
    w = np.full((2, SEQ), 2.0 / NF)
    w[:, 0] = 1.0 / NF
    inv = (tab * w[:, None, :]).transpose(0, 2, 1).reshape(2, NT, P, NT, P)
    c["c_idft"] = np.ascontiguousarray(inv.transpose(3, 2, 0, 1, 4).reshape(NT, P, 2 * NT, P)).astype(f32)
    tt = np.linspace(0.0, 1.0, SEQ, dtype=f32)
    ang = (f32(2 * np.pi) * np.arange(SEQ, dtype=f32) / f32(SEQ))[:, None] * np.linspace(1e-4, 15, 16, dtype=f32)[None]
    c["c_feats"] = np.ascontiguousarray(np.concatenate([tt[:, None], np.cos(ang), -np.sin(ang)], 1).T.astype(f32))
    lo, hi = np.log(1e-2) / 1.5, np.log(1e-2) / 0.3
    deltas = np.abs(np.linspace(lo, hi, HY_W, dtype=f32))
    c["c_window"] = np.exp(-tt[:, None] * deltas[None]).astype(f32)
    return c


def load_constants(nc, pairs):
    with Stage(nc, "init") as s:
        got = s.sem("got")
        block = s.block()

        @block.sync
        def _(sp):
            for dst, src in pairs:
                sp.dma_start(dst, src).then_inc(got, 16)
            sp.wait_ge(got, 16 * len(pairs))


def halves(nc, own, name):
    return [own.enter_context(nc.sbuf_tensor(f"{name}_{half}", [P, D // P, SEQ], HALF)) for half in ("hi", "lo")]


def first_layer(nc, A, C, scratch):
    w_in = A["w_in"]
    conv1, z, vo = scratch("conv1", [CONV1, SEQ]), scratch("z", [SEQ, SSD_W]), scratch("vo", [SEQ, 2 * ML_W])
    gate_tab, m_rows, mix = scratch("gate_tab", [SEQ, GATE_COLS]), scratch("m_rows", [ML_H, SEQ]), scratch("mix", [SEQ, MIX_W])
    with ExitStack() as own:
        small = own.enter_context(nc.sbuf_tensor("small", [P, NT, SSD_H + 2 * ML_H], F32))
        with ExitStack() as own2:
            hT = halves(nc, own2, "h1T")
            w_few = own2.enter_context(nc.sbuf_tensor("gate_w", [P, D // P, SSD_H + 2 * ML_H], F32))
            residual_norm(nc, "n1", A["x"], A["norm1_w"], C["ident"], hT,
                          also=[(w_few[:, :, 0:SSD_H], rows(w_in[:, O_DT:O_DT + SSD_H])),
                                (w_few[:, :, SSD_H:], rows(w_in[:, O_IF:O_IF + 2 * ML_H]))])
            small_gemm(nc, "sg", hT, D // P, w_few, C["ident"], small)
            par = A["params1"]
            gemm(nc, "g1", hT, D // P, [
                dict(kind="conv", taps=4, left=3, silu=True, w=w_in[:, O_XBC:O_XBC + XBC], params=par[0:XBC], out=conv1[0:XBC]),
                dict(kind="conv", taps=4, left=3, silu=True, w=w_in[:, O_QK:O_QK + 2 * ML_W], params=par[XBC:], out=conv1[XBC:]),
                dict(kind="tok", w=w_in[:, 0:SSD_W], out=z),
                dict(kind="tok", w=w_in[:, O_V:O_V + 2 * ML_W], out=vo)], clear=scratch("xs"))
        gates(nc, small, A["ssd_dt_bias"], A["ssd_a_log"], A["ml_i_bias"], A["ml_f_bias"], C["ident"], gate_tab, m_rows)
    ssd(nc, conv1, z, gate_tab, A["ssd_d"], A["ssd_norm_w"], C["ident"], C["tri"], C["ones"], C["neg"], mix)
    mlstm(nc, conv1, vo, gate_tab, m_rows, A["ml_norm_w"], C["ident"], C["ones"], C["neg"], mix)
    proj, x1, h2 = scratch("proj", [SEQ, D]), scratch("x1", [SEQ, D]), scratch("h2", [SEQ, D])
    with ExitStack() as own:
        mixT = own.enter_context(nc.sbuf_tensor("mixT", [P, MIX_W // P, SEQ], F32))
        transpose_in(nc, "tm", mix, mixT, C["ident"])
        gemm_deep(nc, "go", mixT, A["w_out"], proj)
    xs, ys, moe, x2 = scratch("xs"), scratch("ys", [N_TILE * P, D]), scratch("moe", [SEQ, D]), scratch("x2", [SEQ, D])
    with ExitStack() as own:
        def mem(name, shape, dt=F32):
            return own.enter_context(nc.sbuf_tensor(name, shape, dt))
        logits, gate2 = mem("logits", [P, NT, N_GROUP + N_EXP]), mem("gate2", [P, NT, 2])
        slots, tile_exp = mem("slots", [P, 2, NT], U32), mem("tile_exp", [P, N_LIST + 1], I32)
        with ExitStack() as own2:
            hT = halves(nc, own2, "h2T")
            w_few = own2.enter_context(nc.sbuf_tensor("router_w", [P, D // P, N_GROUP + N_EXP], F32))
            residual_norm(nc, "n2", A["x"], A["norm2_w"], C["ident"], hT, add=proj, sum_out=x1, y_out=h2,
                          also=[(w_few[:, :, 0:N_GROUP], rows(A["router_g_w"])), (w_few[:, :, N_GROUP:], rows(A["router_e_w"]))])
            small_gemm(nc, "rl", hT, D // P, w_few, C["ident"], logits)
        route(nc, logits, A["router_g_b"], A["router_e_b"], C["strict"], C["ones"], A["c_iota"], h2, xs, gate2, slots,
              tile_exp, C["ident"])
        experts(nc, xs, ys, A["exp_w_gate"], A["exp_w_up"], A["exp_w_down"], tile_exp, C["ident"])
        combine(nc, ys, gate2, slots, moe)
    return x1, moe, x2


def second_layer(nc, A, C, scratch, x1, moe, x2, out):
    w_in = A["w_in_2"]
    n_conv = 7 * 512
    par, conv2, gates2 = scratch("par2", [n_conv, 5]), scratch("conv2", [n_conv, SEQ]), scratch("gates2", [SEQ, 2 * D])
    conv_params(nc, A["hy_conv_w_2"], A["hy_conv_b_2"], A["rw_mu_2"], par)
    with ExitStack() as own:
        xT = halves(nc, own, "x2T")
        residual_norm(nc, "nf", x1, A["norm_f_w"], C["ident"], xT, add=moe, y_out=x2)
        gemm(nc, "g2", xT, D // P, [
            dict(kind="conv", taps=3, left=1, silu=False, w=w_in[:, 0:n_conv], params=par, out=conv2),
            dict(kind="tok", w=w_in[:, CONV2:CONV2 + 2 * D], out=gates2)])
    sums, spec = scratch("sums", [2, 2, SEQ, HY_W]), scratch("spec", [2, NT, 2, P, HY_W])
    hyena_filters(nc, A["c_feats"], A["c_window"], A["hy_filt_w1_2"], A["hy_filt_b1_2"], A["hy_filt_w2_2"],
                  A["hy_filt_b2_2"], A["hy_filt_w3_2"], A["hy_filt_b3_2"], A["hy_filt_w4_2"], A["hy_sin_freq_2"], sums)
    for o in range(2):
        filter_spectrum(nc, f"fs{o}", sums[o], A["c_dft"], spec[o])
    hy, rw = scratch("hy", [SEQ, HY_W]), scratch("rw", [SEQ, RW_W])
    hyena(nc, conv2, spec, A["hy_skip_2"], A["c_dft"], A["c_idft"], C["ident"], hy)
    vecs, v_tok, half = scratch("vecs", [2, SEQ, RK, RW_W]), scratch("v_tok", [SEQ, RW_W]), scratch("half", [2, NCH, RW_W])
    bonus, g_tok, y_rw = scratch("bonus", [SEQ, RW_W]), scratch("g_tok", [SEQ, RW_W]), scratch("y_rw", [2, SEQ, RW_W])
    rw_prepare(nc, conv2, A["rw_w0_2"], A["rw_w2_2"], A["rw_a0_2"], A["rw_a2_2"], A["rw_g2_2"], A["rw_k_k_2"],
               A["rw_k_a_2"], A["rw_r_k_2"].rearrange("h d -> (h d)"), C["tri"], C["low"], C["ones"], C["ident"],
               vecs, v_tok, half, bonus, g_tok)
    rw_scan(nc, vecs, v_tok, half, A["c_masks"], A["c_nmasks"], C["ident"], y_rw)
    rw_finish(nc, y_rw, bonus, g_tok, A["rw_gn_w_2"], A["rw_gn_b_2"], rw)
    yh, yr, mo, x3, fo = (scratch(n, [SEQ, D]) for n in ("yh", "yr", "mo", "x3", "fo"))
    for name, src, w, dst in (("h", hy, A["w_hy_out_2"], yh), ("r", rw, A["w_rw_out_2"], yr)):
        with ExitStack() as own:
            sT = own.enter_context(nc.sbuf_tensor(f"s{name}T", [P, HY_W // P, SEQ], F32))
            transpose_in(nc, f"ti{name}", src, sT, C["ident"])
            gemm_deep(nc, f"gm{name}", sT, w, dst)
    with ExitStack() as own:
        mT = own.enter_context(nc.sbuf_tensor("mT", [P, D // P, SEQ], F32))
        gate_mix(nc, "mx", gates2, yh, yr, C["ident"], mT)
        gemm_deep(nc, "gw", mT, A["w_o_2"], mo)
    with ExitStack() as own:
        xT = halves(nc, own, "x3T")
        residual_norm(nc, "l1", x2, A["ln1_w_2"], C["ident"], xT, alpha=DN_ALPHA, add=mo, bias=A["ln1_b_2"],
                      eps=LN_EPS, y_out=x3)
        hid = own.enter_context(nc.sbuf_tensor("hid", [P, FFN_H // P, SEQ], F32))
        ffn_up(nc, xT, A["ffn_w_gate_2"], A["ffn_w_up_2"], hid)
        gemm_deep(nc, "fd", hid, A["ffn_w_down_2"], fo, n_out=2)
    residual_norm(nc, "l2", x3, A["ln2_w_2"], C["ident"], None, alpha=DN_ALPHA, add=fo, bias=A["ln2_b_2"],
                  eps=LN_EPS, y_out=out)


def build(nc, A, out):
    made = {}

    def scratch(name, shape=None):
        if shape is not None:
            made[name] = nc.dram_tensor(f"s_{name}", shape, F32, kind="Internal").ap()
        return made[name]

    with ExitStack() as ctx:
        names = ("ident", "tri", "strict", "ones", "neg", "low")
        C = {n: ctx.enter_context(nc.sbuf_tensor(f"k_{n}", [P, P], F32))[:, :] for n in names}
        xs = scratch("xs", [N_SLOT, D])
        load_constants(nc, [(C[n], A[f"c_{n}"]) for n in names])
        x1, moe, x2 = first_layer(nc, A, C, scratch)
        second_layer(nc, A, C, scratch, x1, moe, x2, out)


_LAYER_INS = [
    "norm1_w", "w_in", "ssd_dt_bias", "ssd_a_log", "ssd_d", "ssd_norm_w", "ml_i_bias", "ml_f_bias", "ml_norm_w", "w_out",
    "norm2_w", "router_g_w", "router_g_b", "router_e_w", "router_e_b", "exp_w_gate", "exp_w_up", "exp_w_down",
    "w_in_2", "hy_conv_w_2", "hy_conv_b_2", "hy_filt_w1_2", "hy_filt_b1_2", "hy_filt_w2_2", "hy_filt_b2_2",
    "hy_filt_w3_2", "hy_filt_b3_2", "hy_filt_w4_2", "hy_sin_freq_2", "hy_skip_2", "rw_mu_2", "rw_w0_2",
    "rw_w2_2", "rw_a0_2", "rw_a2_2", "rw_g2_2", "rw_k_k_2", "rw_k_a_2", "rw_r_k_2", "rw_gn_w_2", "rw_gn_b_2",
    "w_hy_out_2", "w_rw_out_2", "w_o_2", "ln1_w_2", "ln1_b_2", "ffn_w_gate_2", "ffn_w_up_2", "ffn_w_down_2",
    "ln2_w_2", "ln2_b_2",
]


def kernel(**inputs):
    import concourse.bacc as _bacc
    from concourse.bass_utils import run_bass_kernel_spmd as _run

    arrays = {"x": inputs["x"][0], "norm_f_w": inputs["norm_f_w"]}
    for name in _LAYER_INS:
        arrays[name] = inputs[name][0]
    scale = np.ones((CONV1, 1), np.float32)
    scale[XBC + ML_W:] = ML_D ** -0.5
    arrays["params1"] = np.concatenate([
        np.concatenate([np.asarray(inputs["ssd_conv_w"][0]).T, np.asarray(inputs["ml_conv_w"][0]).T], 0),
        np.concatenate([np.asarray(inputs["ssd_conv_b"][0]), np.asarray(inputs["ml_conv_b"][0])])[:, None], scale], 1)
    arrays.update(constants())
    nc = _bacc.Bacc("TRN2", target_bir_lowering=False, num_devices=1)
    fed, aps = {}, {}
    for name, a in arrays.items():
        a = np.ascontiguousarray(a)
        fed[f"in_{name}"] = a
        aps[name] = nc.dram_tensor(f"in_{name}", a.shape, mybir.dt.from_np(a.dtype), kind="ExternalInput").ap()
    out = nc.dram_tensor("out", (SEQ, D), F32, kind="ExternalOutput").ap()
    build(nc, aps, out)
    r = _run(nc, [fed], core_ids=[0])
    return r.results[0]["out"].reshape(1, SEQ, D)
```
